# Optimizing a Trainium2 kernel written in Bass

```python
import math
import jax
import jax.numpy as jnp
from jax import lax
import numpy as np
import jax, jax.numpy as jnp

D_MODEL = 1024
BATCH = 1
SEQ = 256
DEPTH = 1

N_META = 16
D_MIX = 2 * D_MODEL
EPS = 1e-6
HG_WIDTH = D_MIX // 2
HG_DK = 128
HG_HEADS = HG_WIDTH // 128
HG_DV = HG_WIDTH // HG_HEADS
HG_KEY = HG_HEADS * HG_DK
HG_CHUNK = 16
M2_WIDTH = D_MIX - HG_WIDTH
M2_HEADDIM = 64
M2_HEADS = M2_WIDTH // M2_HEADDIM
M2_STATE = 128
M2_GROUPS = 2
M2_HPG = M2_HEADS // M2_GROUPS
M2_GN = M2_GROUPS * M2_STATE
M2_XBC = M2_WIDTH + 2 * M2_GN
M2_CONV = 4
M2_CHUNK = 64
DT_MIN = 1e-3
DT_MAX = 1e-1
D_FF = 2816
FFN_CONV = 3
PROJ_SIZES = (HG_KEY, HG_KEY, HG_WIDTH, HG_WIDTH, M2_WIDTH, M2_XBC, M2_HEADS)
D_PROJ = sum(PROJ_SIZES)
PROJ_SPLITS = tuple(int(v) for v in np.cumsum(PROJ_SIZES)[:-1])


def rmsnorm(x, w):
    xf = x.astype(jnp.float32)
    y = xf * lax.rsqrt(jnp.mean(xf * xf, axis=-1, keepdims=True) + EPS)
    return (y * w.astype(jnp.float32)).astype(x.dtype)

def causal_dwconv(x, w, b):
    k_taps, length = w.shape[0], x.shape[1]
    xp = jnp.pad(x, ((0, 0), (k_taps - 1, 0), (0, 0)))
    y = b + xp[:, 0:length] * w[0]
    for k in range(1, k_taps):
        y = y + xp[:, k:k + length] * w[k]
    return y

def front_pad(t, n):
    return jnp.pad(t, ((0, 0), (n, 0)) + ((0, 0),) * (t.ndim - 2))

def to_chunks(t, c):
    return t.reshape((t.shape[0], t.shape[1] // c, c) + t.shape[2:])

def hgrn2_mixer(q, f_pre, i_in, g, lb, norm_w):
    bsz, length, _ = q.shape
    f32 = jnp.float32
    f = lb + (1.0 - lb) * jax.nn.sigmoid(f_pre.astype(f32))
    k = 1.0 - f
    log_f = jnp.log(f)
    qa = jax.nn.silu(q.astype(f32))
    pad = (-N_META) % HG_CHUNK
    lp = length + pad

    def prep(t, d):
        return to_chunks(front_pad(t, pad).reshape(bsz, lp, HG_HEADS, d), HG_CHUNK)

    qc, kc, gc = prep(qa, HG_DK), prep(k, HG_DK), prep(log_f, HG_DK)
    vc = prep(i_in.astype(f32), HG_DV)
    bcum = jnp.cumsum(gc, axis=2)
    blast = bcum[:, :, -1]
    q_dec = qc * jnp.exp(bcum)
    k_inv = kc * jnp.exp(-bcum)
    k_end = kc * jnp.exp(blast[:, :, None] - bcum)
    causal = jnp.tril(jnp.ones((HG_CHUNK, HG_CHUNK), dtype=bool))
    scores = jnp.einsum('bnrhk,bnshk->bnhrs', q_dec, k_inv)
    scores = jnp.where(causal, scores, 0.0)
    o_intra = jnp.einsum('bnhrs,bnshv->bnrhv', scores, vc)

    def step(state, inp):
        q_n, k_n, v_n, d_n = inp
        o_n = jnp.einsum('brhk,bhkv->brhv', q_n, state)
        state = d_n[..., None] * state + jnp.einsum('brhk,brhv->bhkv', k_n, v_n)
        return state, o_n

    s0 = jnp.zeros((bsz, HG_HEADS, HG_DK, HG_DV), f32)
    xs = (jnp.moveaxis(q_dec, 1, 0), jnp.moveaxis(k_end, 1, 0),
          jnp.moveaxis(vc, 1, 0), jnp.moveaxis(jnp.exp(blast), 1, 0))
    _, o_inter = lax.scan(step, s0, xs)
    o = o_intra + jnp.moveaxis(o_inter, 0, 1)
    o = o.reshape(bsz, lp, HG_HEADS, HG_DV)[:, pad:]
    o = o * lax.rsqrt(jnp.mean(o * o, axis=-1, keepdims=True) + EPS)
    o = o.reshape(bsz, length, HG_WIDTH) * norm_w.astype(f32)
    return (o * jax.nn.silu(g.astype(f32))).astype(q.dtype)

def mamba2_mixer(z, xbc, dt_pre, conv_w, conv_b, dt_bias, a_log, d_skip, norm_w):
    bsz, length, _ = z.shape
    f32 = jnp.float32
    xbc = jax.nn.silu(causal_dwconv(xbc, conv_w, conv_b).astype(f32))
    x_in = xbc[..., :M2_WIDTH].reshape(bsz, length, M2_GROUPS, M2_HPG, M2_HEADDIM)
    b_in = xbc[..., M2_WIDTH:M2_WIDTH + M2_GN].reshape(bsz, length, M2_GROUPS, M2_STATE)
    c_in = xbc[..., M2_WIDTH + M2_GN:].reshape(bsz, length, M2_GROUPS, M2_STATE)
    dt = jax.nn.softplus(dt_pre.astype(f32) + dt_bias.astype(f32))
    dt = dt.reshape(bsz, length, M2_GROUPS, M2_HPG)
    a = -jnp.exp(a_log.astype(f32)).reshape(M2_GROUPS, M2_HPG)
    da = dt * a
    xdt = x_in * dt[..., None]
    pad = (-N_META) % M2_CHUNK
    lp = length + pad
    xc = to_chunks(front_pad(xdt, pad), M2_CHUNK)
    ac = to_chunks(front_pad(da, pad), M2_CHUNK)
    bc = to_chunks(front_pad(b_in, pad), M2_CHUNK)
    cc = to_chunks(front_pad(c_in, pad), M2_CHUNK)
    a_cum = jnp.cumsum(ac, axis=2)
    causal = jnp.tril(jnp.ones((M2_CHUNK, M2_CHUNK), dtype=bool))
    seg = a_cum[:, :, :, None] - a_cum[:, :, None, :]
    l_mat = jnp.exp(jnp.where(causal[:, :, None, None], seg, -jnp.inf))
    cb = jnp.einsum('bnigs,bnjgs->bnijg', cc, bc)
    y_diag = jnp.einsum('bnijgh,bnjghp->bnighp', cb[..., None] * l_mat, xc)
    decay_to_end = jnp.exp(a_cum[:, :, -1:] - a_cum)
    u = jnp.einsum('bnjgs,bnjghp->bnghps', bc, xc * decay_to_end[..., None])
    chunk_decay = jnp.exp(a_cum[:, :, -1])

    def step(state, inp):
        c_n, e_n, u_n, d_n = inp
        y_n = jnp.einsum('bigs,bghps->bighp', c_n, state) * e_n[..., None]
        state = d_n[..., None, None] * state + u_n
        return state, y_n

    s0 = jnp.zeros((bsz, M2_GROUPS, M2_HPG, M2_HEADDIM, M2_STATE), f32)
    xs = (jnp.moveaxis(cc, 1, 0), jnp.moveaxis(jnp.exp(a_cum), 1, 0),
          jnp.moveaxis(u, 1, 0), jnp.moveaxis(chunk_decay, 1, 0))
    _, y_off = lax.scan(step, s0, xs)
    y = y_diag + jnp.moveaxis(y_off, 0, 1)
    y = y.reshape(bsz, lp, M2_GROUPS, M2_HPG, M2_HEADDIM)[:, pad:]
    y = y + d_skip.astype(f32).reshape(M2_GROUPS, M2_HPG, 1) * x_in
    y = y.reshape(bsz, length, M2_WIDTH) * jax.nn.silu(z.astype(f32))
    yg = y.reshape(bsz, length, M2_GROUPS, M2_WIDTH // M2_GROUPS)
    yg = yg * lax.rsqrt(jnp.mean(yg * yg, axis=-1, keepdims=True) + EPS)
    y = yg.reshape(bsz, length, M2_WIDTH) * norm_w.astype(f32)
    return y.astype(z.dtype)

def conv_glu_ffn(h, w_up, conv_w, conv_b, w_down):
    u = causal_dwconv(h @ w_up, conv_w, conv_b)
    gate, val = jnp.split(u, 2, axis=-1)
    return (jax.nn.silu(gate) * val) @ w_down

def first_inputs(seed: int = 0) -> dict:
    key = jax.random.key(seed)
    ks = jax.random.split(key, 20)
    f32 = jnp.float32

    def nrm(k, shape, scale):
        return scale * jax.random.normal(k, shape, f32)

    def gain(k, shape):
        return 1.0 + 0.05 * jax.random.normal(k, shape, f32)

    dt0 = jnp.exp(jax.random.uniform(ks[8], (DEPTH, M2_HEADS), f32,
                                     minval=math.log(DT_MIN), maxval=math.log(DT_MAX)))
    dt_bias = dt0 + jnp.log(-jnp.expm1(-dt0))
    a_log = jnp.log(jax.random.uniform(ks[9], (DEPTH, M2_HEADS), f32, minval=1.0, maxval=16.0))
    return {
        'x': nrm(ks[0], (BATCH, SEQ, D_MODEL), 1.0),
        'meta_tokens': nrm(ks[1], (N_META, D_MODEL), 1.0),
        'norm1_w': gain(ks[2], (DEPTH, D_MODEL)),
        'w_in': nrm(ks[3], (DEPTH, D_MODEL, D_PROJ), D_MODEL ** -0.5),
        'hg_lb_logits': nrm(ks[4], (DEPTH + 1, HG_KEY), 0.1),
        'hg_norm_w': gain(ks[5], (DEPTH, HG_WIDTH)),
        'm2_conv_w': nrm(ks[6], (DEPTH, M2_CONV, M2_XBC), M2_CONV ** -0.5),
        'm2_conv_b': nrm(ks[7], (DEPTH, M2_XBC), 0.02),
        'm2_dt_bias': dt_bias,
        'm2_a_log': a_log,
        'm2_d': gain(ks[10], (DEPTH, M2_HEADS)),
        'm2_norm_w': gain(ks[11], (DEPTH, M2_WIDTH)),
        'w_out': nrm(ks[12], (DEPTH, D_MIX, D_MODEL), D_MIX ** -0.5),
        'norm2_w': gain(ks[13], (DEPTH, D_MODEL)),
        'ffn_w_up': nrm(ks[14], (DEPTH, D_MODEL, 2 * D_FF), D_MODEL ** -0.5),
        'ffn_conv_w': nrm(ks[15], (DEPTH, FFN_CONV, 2 * D_FF), FFN_CONV ** -0.5),
        'ffn_conv_b': nrm(ks[16], (DEPTH, 2 * D_FF), 0.02),
        'ffn_w_down': nrm(ks[17], (DEPTH, D_FF, D_MODEL), D_FF ** -0.5),
        'final_norm_w': gain(ks[18], (D_MODEL,)),
    }

def first_block(x, meta_tokens, norm1_w, w_in, hg_lb_logits, hg_norm_w, m2_conv_w, m2_conv_b,
              m2_dt_bias, m2_a_log, m2_d, m2_norm_w, w_out, norm2_w, ffn_w_up, ffn_conv_w,
              ffn_conv_b, ffn_w_down, final_norm_w):
    bsz = x.shape[0]
    meta = jnp.broadcast_to(meta_tokens.astype(x.dtype)[None], (bsz, N_META, D_MODEL))
    h = jnp.concatenate([meta, x], axis=1)
    lbs = jnp.cumsum(jax.nn.softmax(hg_lb_logits.astype(jnp.float32), axis=0), axis=0)
    for l in range(DEPTH):
        u = rmsnorm(h, norm1_w[l])
        proj = u @ w_in[l]
        hg_q, hg_f, hg_i, hg_g, m2_z, m2_xbc, m2_dt = jnp.split(proj, PROJ_SPLITS, axis=-1)
        out_a = hgrn2_mixer(hg_q, hg_f, hg_i, hg_g, lbs[l], hg_norm_w[l])
        out_b = mamba2_mixer(m2_z, m2_xbc, m2_dt, m2_conv_w[l], m2_conv_b[l], m2_dt_bias[l],
                             m2_a_log[l], m2_d[l], m2_norm_w[l])
        h = h + jnp.concatenate([out_a, out_b], axis=-1) @ w_out[l]
        h = h + conv_glu_ffn(rmsnorm(h, norm2_w[l]), ffn_w_up[l], ffn_conv_w[l],
                             ffn_conv_b[l], ffn_w_down[l])
    y = rmsnorm(h, final_norm_w)
    return y[:, N_META:, :]


HEAD_DIM = 64
N_ATT_HEADS = 6
N_KV_GROUPS = 2
ATT_WIDTH = N_ATT_HEADS * HEAD_DIM
KV_WIDTH = N_KV_GROUPS * HEAD_DIM
N_IDX_HEADS = 8
IDX_DIM = 32
TOPK_MAX = 256
Q_BLOCK = 128
CONV_CHANNELS = 384
SHORT_CONV_K = 3
N_CROSS_HEADS = 4
CROSS_WIDTH = N_CROSS_HEADS * HEAD_DIM
MEM_LEN = 256
N_BRANCHES = 3
FFN_CONV_K = 3
ROPE_THETA = 500000.0
ROPE_FRACTION = 4
NORM_EPS = 1e-6

PROJ_SIZES_2 = (ATT_WIDTH, KV_WIDTH, KV_WIDTH, N_IDX_HEADS * IDX_DIM, IDX_DIM, N_IDX_HEADS,
              3 * CONV_CHANNELS, CROSS_WIDTH, N_BRANCHES * D_MODEL)
PROJ_WIDTH = sum(PROJ_SIZES_2)


def rms_norm(x, g):
    xf = x.astype(jnp.float32)
    y = xf * lax.rsqrt(jnp.mean(xf * xf, axis=-1, keepdims=True) + NORM_EPS)
    return (y * g.astype(jnp.float32)).astype(x.dtype)

def split_cols(a, sizes):
    out, off = [], 0
    for n in sizes:
        out.append(a[..., off:off + n])
        off += n
    return out

def rope_tables(positions, rot_dim, dtype):
    half = rot_dim // 2
    inv_freq = ROPE_THETA ** (-jnp.arange(half, dtype=jnp.float32) / half)
    ang = positions.astype(jnp.float32)[:, None] * inv_freq[None, :]
    return jnp.cos(ang).astype(dtype), jnp.sin(ang).astype(dtype)

def partial_rope(x, cos, sin):
    half = cos.shape[-1]
    shape = (1, cos.shape[0]) + (1,) * (x.ndim - 3) + (half,)
    c, s = cos.reshape(shape), sin.reshape(shape)
    x1, x2, rest = x[..., :half], x[..., half:2 * half], x[..., 2 * half:]
    return jnp.concatenate([x1 * c - x2 * s, x2 * c + x1 * s, rest], axis=-1)

def causal_dwconv_2(u, w):
    k, c = w.shape
    return lax.conv_general_dilated(u, w[:, None, :].astype(u.dtype), window_strides=(1,),
                                    padding=[(k - 1, 0)],
                                    dimension_numbers=("NWC", "WIO", "NWC"),
                                    feature_group_count=c)

def dsa_attention(q, k, v, qi, ki, wi):
    b, s = q.shape[:2]
    topk = min(TOPK_MAX, s // 4)
    blk = min(Q_BLOCK, s)
    nb = s // blk
    rep = N_ATT_HEADS // N_KV_GROUPS
    idx_scale = (N_IDX_HEADS * IDX_DIM) ** -0.5
    att_scale = HEAD_DIM ** -0.5
    key_pos = jnp.arange(s)
    gather = jax.vmap(lambda a, i: a[i])

    def to_blocks(a):
        return jnp.moveaxis(a.reshape((b, nb, blk) + a.shape[2:]), 1, 0)

    def one_block(args):
        q_b, qi_b, wi_b, start = args
        qpos = start + jnp.arange(blk)
        causal = key_pos[None, :] <= qpos[:, None]
        rel = jax.nn.relu(jnp.einsum('bqhd,bsd->bqhs', qi_b, ki).astype(jnp.float32))
        score = jnp.einsum('bqh,bqhs->bqs', wi_b.astype(jnp.float32), rel) * idx_scale
        score = jnp.where(causal[None], score, -jnp.inf)
        _, sel = lax.top_k(score, topk)
        k_sel = gather(k, sel)
        v_sel = gather(v, sel)
        qg = q_b.reshape(b, blk, N_KV_GROUPS, rep, HEAD_DIM)
        logits = jnp.einsum('bqgrd,bqkgd->bqgrk', qg, k_sel).astype(jnp.float32) * att_scale
        valid = sel <= qpos[None, :, None]
        logits = jnp.where(valid[:, :, None, None, :], logits, -jnp.inf)
        p = jax.nn.softmax(logits, axis=-1).astype(v.dtype)
        o = jnp.einsum('bqgrk,bqkgd->bqgrd', p, v_sel)
        return o.reshape(b, blk, N_ATT_HEADS * HEAD_DIM)

    starts = jnp.arange(nb) * blk
    out = lax.map(one_block, (to_blocks(q), to_blocks(qi), to_blocks(wi), starts))
    return jnp.moveaxis(out, 0, 1).reshape(b, s, N_ATT_HEADS * HEAD_DIM)

def memory_attention(qc, km, vm):
    b, s = qc.shape[:2]
    logits = jnp.einsum('bshd,bmhd->bhsm', qc, km).astype(jnp.float32) * HEAD_DIM ** -0.5
    p = jax.nn.softmax(logits, axis=-1).astype(vm.dtype)
    return jnp.einsum('bhsm,bmhd->bshd', p, vm).reshape(b, s, CROSS_WIDTH)

def second_inputs(seed: int = 0) -> dict:
    key = jax.random.key(seed)
    ks = jax.random.split(key, 20)

    def w(k, shape, fan_in):
        return jax.random.normal(k, shape, jnp.float32) * fan_in ** -0.5

    def gain(k, shape):
        return 1.0 + 0.02 * jax.random.normal(k, shape, jnp.float32)

    return {
        "x": jax.random.normal(ks[0], (BATCH, SEQ, D_MODEL), jnp.float32),
        "mem": jax.random.normal(ks[1], (BATCH, MEM_LEN, D_MODEL), jnp.float32),
        "g_mix": gain(ks[2], (DEPTH, D_MODEL)),
        "w_in": w(ks[3], (DEPTH, D_MODEL, PROJ_WIDTH), D_MODEL),
        "b_gate": 0.02 * jax.random.normal(ks[4], (DEPTH, N_BRANCHES * D_MODEL), jnp.float32),
        "conv_w_short": w(ks[5], (DEPTH, SHORT_CONV_K, CONV_CHANNELS), SHORT_CONV_K),
        "w_att_out": w(ks[6], (DEPTH, ATT_WIDTH, D_MODEL), ATT_WIDTH),
        "w_conv_out": w(ks[7], (DEPTH, CONV_CHANNELS, D_MODEL), CONV_CHANNELS),
        "w_mem_out": w(ks[8], (DEPTH, CROSS_WIDTH, D_MODEL), CROSS_WIDTH),
        "w_o": w(ks[9], (DEPTH, D_MODEL, D_MODEL), D_MODEL),
        "g_mem": gain(ks[10], (DEPTH, D_MODEL)),
        "w_mem_kv": w(ks[11], (DEPTH, D_MODEL, 2 * CROSS_WIDTH), D_MODEL),
        "g_ffn": gain(ks[12], (DEPTH, D_MODEL)),
        "w_up": w(ks[13], (DEPTH, D_MODEL, 2 * D_FF), D_MODEL),
        "conv_w_ffn": w(ks[14], (DEPTH, FFN_CONV_K, 2 * D_FF), FFN_CONV_K),
        "w_down": w(ks[15], (DEPTH, D_FF, D_MODEL), D_FF),
        "g_final": gain(ks[16], (D_MODEL,)),
    }

def second_block(x, mem, g_mix, w_in, b_gate, conv_w_short, w_att_out, w_conv_out, w_mem_out,
              w_o, g_mem, w_mem_kv, g_ffn, w_up, conv_w_ffn, w_down, g_final):
    b, s, d = x.shape
    m = mem.shape[1]
    positions = jnp.arange(s)
    cos_a, sin_a = rope_tables(positions, HEAD_DIM // ROPE_FRACTION, x.dtype)
    cos_i, sin_i = rope_tables(positions, IDX_DIM // ROPE_FRACTION, x.dtype)

    for l in range(DEPTH):
        h = rms_norm(x, g_mix[l])
        proj = h @ w_in[l]
        q, k, v, qi, ki, wi, conv_in, qc, gate_pre = split_cols(proj, PROJ_SIZES_2)

        q = partial_rope(q.reshape(b, s, N_ATT_HEADS, HEAD_DIM), cos_a, sin_a)
        k = partial_rope(k.reshape(b, s, N_KV_GROUPS, HEAD_DIM), cos_a, sin_a)
        v = v.reshape(b, s, N_KV_GROUPS, HEAD_DIM)
        qi = partial_rope(qi.reshape(b, s, N_IDX_HEADS, IDX_DIM), cos_i, sin_i)
        ki = partial_rope(ki, cos_i, sin_i)
        y_att = dsa_attention(q, k, v, qi, ki, wi) @ w_att_out[l]

        bg, cg, u = jnp.split(conv_in, 3, axis=-1)
        y_conv = (bg * causal_dwconv_2(cg * u, conv_w_short[l])) @ w_conv_out[l]

        mem_kv = (rms_norm(mem, g_mem[l]) @ w_mem_kv[l]).reshape(b, m, 2, N_CROSS_HEADS, HEAD_DIM)
        y_mem = memory_attention(qc.reshape(b, s, N_CROSS_HEADS, HEAD_DIM),
                                 mem_kv[:, :, 0], mem_kv[:, :, 1]) @ w_mem_out[l]

        gates = jax.nn.sigmoid(gate_pre + b_gate[l]).reshape(b, s, N_BRANCHES, d)
        merged = gates[:, :, 0] * y_att + gates[:, :, 1] * y_conv + gates[:, :, 2] * y_mem
        x = x + merged @ w_o[l]

        h = rms_norm(x, g_ffn[l])
        up = causal_dwconv_2(h @ w_up[l], conv_w_ffn[l])
        gate, val = jnp.split(up, 2, axis=-1)
        x = x + (jax.nn.silu(gate) * val) @ w_down[l]

    return rms_norm(x, g_final)


def setup_inputs(seed=0):
    out = dict(first_inputs(seed))
    for name, value in second_inputs(seed + 1).items():
        if name != "x":
            out[name + "_2"] = value
    return out


def reference(
    x, meta_tokens, norm1_w, w_in, hg_lb_logits, hg_norm_w, m2_conv_w, m2_conv_b, m2_dt_bias,
    m2_a_log, m2_d, m2_norm_w, w_out, norm2_w, ffn_w_up, ffn_conv_w, ffn_conv_b, ffn_w_down,
    final_norm_w, mem_2, g_mix_2, w_in_2, b_gate_2, conv_w_short_2, w_att_out_2, w_conv_out_2,
    w_mem_out_2, w_o_2, g_mem_2, w_mem_kv_2, g_ffn_2, w_up_2, conv_w_ffn_2, w_down_2, g_final_2,
):
    x = first_block(
        x, meta_tokens, norm1_w, w_in, hg_lb_logits, hg_norm_w, m2_conv_w, m2_conv_b,
        m2_dt_bias, m2_a_log, m2_d, m2_norm_w, w_out, norm2_w, ffn_w_up, ffn_conv_w, ffn_conv_b,
        ffn_w_down, final_norm_w,
    )
    return second_block(
        x, mem_2, g_mix_2, w_in_2, b_gate_2, conv_w_short_2, w_att_out_2, w_conv_out_2,
        w_mem_out_2, w_o_2, g_mem_2, w_mem_kv_2, g_ffn_2, w_up_2, conv_w_ffn_2, w_down_2,
        g_final_2,
    )


_drawn_inputs = setup_inputs


def setup_inputs(seed=0):
    import zlib

    import numpy as np

    out = dict(_drawn_inputs(seed))
    spreads = {}
    factors = {'hg_lb_logits': 6.203,
     'ffn_conv_b': 2.864,
     'b_gate_2': 8.0,
     'g_mem_2': 8.0,
     'g_ffn_2': 4.085,
     'g_final_2': 2.729}
    for name, (base, spread) in spreads.items():
        noise = np.random.default_rng([zlib.crc32(name.encode()), seed]).standard_normal(out[name].shape)
        drawn = base * np.exp(spread * noise) if base else spread * noise
        out[name] = jnp.asarray(drawn.astype(out[name].dtype))
    for name, factor in factors.items():
        out[name] = (out[name] * factor).astype(out[name].dtype)
    return out
```

```python
from contextlib import ExitStack

import numpy as np

P = 128
D = 1024
KD = D // P
META, SEQ = 16, 256
T1 = META + SEQ
T2 = SEQ
FF = 2816
MF = FF // P
HEADS = 8
CHUNK = 16
NCH = T1 // CHUNK
WIN = 2 * CHUNK
M2H = 16
GN = 128
EPS = 1e-6
TOPK = 64
ATT_HEADS, IDX_HEADS, CROSS_HEADS = 6, 8, 4
ROT_A, ROT_I = 8, 4
THETA = 500000.0
FILL = -3.0e38
TAKEN = -3.4e38
PENALTY = -1.0e30

C_Q, C_F, C_I, C_G, C_Z, C_X, C_B, C_C, C_DT = 0, 1024, 2048, 3072, 4096, 5120, 6144, 6400, 6656
C2_Q, C2_K, C2_V, C2_QI, C2_KI, C2_WI, C2_BG, C2_CG, C2_U, C2_QC, C2_GATE = (
    0, 384, 512, 640, 896, 928, 936, 1320, 1704, 2088, 2344)

VEC_PARTS = [("norm1", 8), ("hg_norm", 8), ("m2_conv", 48), ("m2_conv_b", 12), ("m2_norm", 8), ("m2_d", 8),
             ("norm2", 8), ("final1", 8), ("f1_conv", 132), ("f1_conv_b", 44), ("lb", 16), ("b_gate", 24),
             ("short", 9), ("g_mix", 8), ("g_mem", 8), ("g_ffn", 8), ("f2_conv", 132), ("g_final", 8)]
VEC, NVEC = {}, 0
for _n, _w in VEC_PARTS:
    VEC[_n] = NVEC
    NVEC += _w

CON_PARTS = [("ident", P), ("ones", T1), ("reset", 2 * T1), ("eps", 1),
             ("rot_a", P), ("rot_i", P), ("cos_a", T2), ("sin_a", T2), ("cos_i", T2), ("sin_i", T2)]
CON, NCON = {}, 0
for _n, _w in CON_PARTS:
    CON[_n] = NCON
    NCON += _w
NCON1 = CON["rot_a"]


def constants():
    c = np.zeros((P, NCON), np.float32)
    c[:, CON["ident"]:CON["ident"] + P] = np.eye(P)
    c[:, CON["ones"]:CON["ones"] + T1] = 1.0
    for rot, cos, sin, half, dim in (("rot_a", "cos_a", "sin_a", ROT_A, 64), ("rot_i", "cos_i", "sin_i", ROT_I, 32)):
        freq = np.float32(THETA) ** (-np.arange(half, dtype=np.float32) / np.float32(half))
        ang = np.arange(T2, dtype=np.float32)[:, None] * freq.astype(np.float32)[None, :]
        c[:, CON[cos]:CON[cos] + T2] = 1.0
        for base in range(0, P, dim):
            for j in range(half):
                a, b = base + j, base + half + j
                for p in (a, b):
                    c[p, CON[cos]:CON[cos] + T2] = np.cos(ang[:, j])
                    c[p, CON[sin]:CON[sin] + T2] = np.sin(ang[:, j])
                c[b, CON[rot] + a] = -1.0
                c[a, CON[rot] + b] = 1.0
    reset = np.ones(2 * T1, np.float32)
    reset[::CHUNK] = 0.0
    c[:, CON["reset"]:CON["reset"] + 2 * T1] = reset
    c[:, CON["eps"]] = EPS
    m = np.zeros((P, T1), np.int32)
    for col in range(T1):
        win, j, r = col // 64, col % 64 // CHUNK, col % CHUNK
        m[32 * j:32 * j + r + 1, col] = 1
    return c, m


def build_program(nc, A, out):
    import concourse.bass as bass
    from concourse import mybir

    F, R, I32 = mybir.dt.float32, mybir.dt.float32r, mybir.dt.int32
    ALU, ACT, AX = mybir.AluOpType, mybir.ActivationFunctionType, mybir.AxisListType
    MUL, ADD, SUB, MAX, MIN = ALU.mult, ALU.add, ALU.subtract, ALU.max, ALU.min
    ctx = ExitStack()
    with ctx:
        queues = {n: [] for n in ("sp", "pe", "act", "dve", "pool")}
        done = {n: ctx.enter_context(nc.semaphore(f"{n}_done")) for n in ("pe", "act", "dve", "pool")}
        count = dict.fromkeys(done, 0)

        def put(engine, issue, after=(), signal=True):
            waits = [t for t in after if t is not None]
            if signal:
                count[engine] += 1
                queues[engine].append((issue, waits, done[engine], 1))
                return done[engine], count[engine]
            queues[engine].append((issue, waits, None, 0))
            return None

        dma_count = {}

        def dma(dst, src, sem, after=(), engine="sp"):
            queues[engine].append((lambda e: e.dma_start(dst, src), [t for t in after if t is not None], sem, 16))
            dma_count[id(sem)] = dma_count.get(id(sem), 0) + 16
            return sem, dma_count[id(sem)]

        def semaphore(name):
            return ctx.enter_context(nc.semaphore(name))

        def mm(o, lhsT, rhs, start, stop, after=(), signal=False):
            return put("pe", lambda e: e.matmul(o, lhsT, rhs, start=start, stop=stop, skip_group_check=True),
                       after, signal)

        def transpose(o, i, ident, after=(), signal=False):
            return put("pe", lambda e: e.transpose(o, i, ident), after, signal)

        def act(o, i, func, after=(), scale=1.0, bias=0.0, accum=None):
            if accum is None:
                return put("act", lambda e: e.activation(o, i, func, bias=bias, scale=scale), after)
            return put("act", lambda e: e.activation(o, i, func, bias=bias, scale=scale, accum_out=accum), after)

        def tt(o, a, b, op, after=(), engine="dve"):
            return put(engine, lambda e: e.tensor_tensor(o, a, b, op), after)

        def ts(o, a, s1, op0, s2=None, op1=None, after=(), engine="dve"):
            if op1 is None:
                return put(engine, lambda e: e.tensor_scalar(o, a, s1, None, op0), after)
            return put(engine, lambda e: e.tensor_scalar(o, a, s1, s2, op0, op1), after)

        def stt(o, a, s, b, op0, op1, after=()):
            return put("dve", lambda e: e.scalar_tensor_tensor(out=o, in0=a, scalar=s, in1=b, op0=op0, op1=op1), after)

        def copy(o, i, after=(), engine="dve"):
            return put(engine, lambda e: e.tensor_copy(o, i), after)

        def memset(o, v, after=(), engine="pool"):
            return put(engine, lambda e: e.memset(o, v), after)

        top = [(nc.sbuf_base + 63) // 64 * 64]
        LIMIT = nc.sbuf_top - 64

        def size(shape):
            return int(np.prod(shape[1:])) * 4

        def place(name, shape, dt, cursor):
            t = nc.alloc_sbuf_tensor_at(name, list(shape), dt, offset=cursor[0])
            cursor[0] += (size(shape) + 63) // 64 * 64
            assert cursor[0] <= LIMIT, (name, cursor[0], LIMIT)
            return t

        def keep(name, shape, dt=F):
            return place(name, shape, dt, top)

        NRAW, NSPLIT, SLAB = 2, 4, 2048
        raw = [keep(f"w_raw{i}", [P, SLAB]) for i in range(NRAW)]
        w_high = [keep(f"w_high{i}", [P, SLAB], R) for i in range(NSPLIT)]
        w_low = [keep(f"w_low{i}", [P, SLAB], R) for i in range(NSPLIT)]
        con = keep("con", [P, NCON1])
        vec = keep("vec", [P, NVEC])
        chunk_mask = keep("chunk_mask", [P, T1], I32)
        heads16 = keep("heads16", [M2H, 8])
        H = keep("H", [P, KD, T1])
        XH = keep("XH", [P, KD, T1], R)
        XL = keep("XL", [P, KD, T1], R)
        NSQ = 4
        SQ = keep("SQ", [P, NSQ, T1])
        rstd = keep("rstd", [P, T1])
        lnv = keep("lnv", [P, T1])

        def con_(name, w, rows=P):
            return con[0:rows, CON[name]:CON[name] + w]

        def vcol(name, i):
            return vec[:, VEC[name] + i:VEC[name] + i + 1]

        ident, ones, eps = con_("ident", P), con_("ones", T1), con_("eps", 1)
        banks = [ctx.enter_context(nc.psum_tensor(f"bank{i}", [P, 512], F)) for i in range(8)]
        bank_free = [None] * 8

        s_first = [semaphore(f"s_first{i}") for i in range(6)]
        t_vec = dma(vec[:], A["vec"], s_first[0])
        t_h = []
        for k in range(0, KD, 4):
            t = dma(H[:, k:k + 4, :], A["hT"].rearrange("(k p) t -> p k t", p=P)[:, k:k + 4, :], s_first[1 + k // 4])
            t_h += [t] * 4
        t_con = dma(con[:], A["con"][:, 0:NCON1], s_first[3], engine="act")
        t_mask = dma(chunk_mask[:], A["chunk_mask"], s_first[4], engine="act")
        t_hd = dma(heads16[:, 0:2], A["heads"], s_first[5], engine="act")

        background = []

        def advance():
            for g in list(background):
                if next(g, "end") == "end":
                    background.remove(g)

        def finish(*gens):
            for g in gens:
                while g in background:
                    advance()

        slabs = []

        class Slab:

            def __init__(self, nk, width, pieces, x, tokens, parts, first=True, last=True, hook=None):
                assert nk * width <= SLAB
                self.nk, self.width, self.pieces = nk, width, pieces
                self.x, self.tokens, self.parts, self.first, self.last, self.hook = x, tokens, parts, first, last, hook
                self.n = len(slabs)
                slabs.append(self)

        s_raw = [semaphore(f"s_raw{i}") for i in range(NRAW)]
        raw_free = [()] * NRAW
        split_free = [None] * NSPLIT
        landed, halves = {}, {}

        def view(t, s):
            return t[:, 0:s.nk * s.width].rearrange("p (k n) -> p k n", k=s.nk)

        def load(n):
            s = slabs[n]
            for i, (c0, w, src, *rows) in enumerate(s.pieces):
                dst = view(raw[n % NRAW], s)[slice(*rows) if rows else slice(0, P), :, c0:c0 + w]
                landed[n] = dma(dst, src, s_raw[n % NRAW], raw_free[n % NRAW] if i == 0 else ())

        lo_engine = lambda n: "dve" if n % 4 == 3 else "pool"

        def split(n):
            s = slabs[n]
            m, q = n % NSPLIT, s.nk * s.width
            r = raw[n % NRAW]
            th = act(w_high[m][:, 0:q], r[:, 0:q], ACT.Copy, [landed[n], split_free[m]])
            tl = tt(w_low[m][:, 0:q], r[:, 0:q], w_high[m][:, 0:q].bitcast(F), SUB, [th, split_free[m]], lo_engine(n))
            raw_free[n % NRAW] = (th, tl)
            halves[n] = (th, tl)

        main_banks = [0, 1, 2]
        turn = [0]
        open_banks = {}
        primed = [0, 0]

        def prime(upto_split):
            while primed[1] < min(upto_split, len(slabs)):
                while primed[0] < min(primed[1] + NRAW, len(slabs)):
                    load(primed[0])
                    primed[0] += 1
                split(primed[1])
                primed[1] += 1
                if primed[0] < min(primed[1] + NRAW, len(slabs)):
                    load(primed[0])
                    primed[0] += 1

        def run(s, steps=1):
            prime(s.n + NSPLIT)
            m = s.n % NSPLIT
            hi, lo = view(w_high[m], s), view(w_low[m], s)
            xh, xl, k0, t0, x_tokens = s.x
            th, tl = halves[s.n]
            tok = None
            for key, c0, M, read in s.parts:
                if s.first:
                    b = main_banks[turn[0] % len(main_banks)]
                    turn[0] += 1
                    open_banks[key] = b
                b = open_banks[key]
                o = banks[b][0:M, 0:s.tokens]
                for k in range(s.nk):
                    x1, x2 = xh[:, k0 + k, t0:t0 + s.tokens], xl[:, k0 + k, t0:t0 + s.tokens]
                    begin, end = s.first and k == 0, s.last and k == s.nk - 1
                    last_of_slab = k == s.nk - 1
                    mm(o, hi[:, k, c0:c0 + M], x1, begin, False, [th, x_tokens[k0 + k][0], bank_free[b] if begin else None])
                    mm(o, hi[:, k, c0:c0 + M], x2, False, False, [x_tokens[k0 + k][1]])
                    tok = mm(o, lo[:, k, c0:c0 + M], x1, False, end, [tl], signal=last_of_slab)
                    if k % 4 == 3 and k != s.nk - 1:
                        for _ in range(steps):
                            advance()
                if s.hook is not None:
                    s.hook()
                    s.hook = None
                if s.last:
                    bank_free[b] = read(banks[b], tok)
                for _ in range(steps):
                    advance()
            split_free[m] = tok

        def columns(w, c, n, k0=0, nk=KD):
            return w[k0 * P:(k0 + nk) * P, c:c + n].rearrange("(k p) n -> p k n", p=P)

        sq_free = [None] * NSQ
        STAT = 7

        def rsqrt_mean(o, total, n, after):
            a = act(lnv[:, 0:o.shape[-1]], total, ACT.Ln, after, scale=1.0 / n, bias=eps)
            return act(o, lnv[:, 0:o.shape[-1]], ACT.Exp, [a], scale=-0.5), a

        def square_sum(h, k, first, last, T, after, held=None, bank=STAT):
            a = act(SQ[:, k % NSQ, 0:T], h, ACT.Square, [after, sq_free[k % NSQ]])

            def on_pe():
                t = mm(banks[bank][:, 0:T], ones[:, 0:P], SQ[:, k % NSQ, 0:T], first, last,
                       [a, t_con, bank_free[bank] if first else None], signal=True)
                sq_free[k % NSQ] = t
                return t
            if held is None:
                return on_pe()
            held.append(on_pe)
            return None

        def scaled_parts(k, h, gain, T, after, free=None, hi=None, lo=None):
            hi, lo = hi or XH, lo or XL
            a = act(hi[:, k, 0:T], h, ACT.Copy, [after, free], scale=gain)
            b = stt(lo[:, k, 0:T], h, gain, hi[:, k, 0:T].bitcast(F), MUL, SUB, [a])
            return a, b

        def parts_of(k, v, hi, lo, after, T, scale=None):
            if scale is None:
                a = act(hi[:, k, 0:T], v, ACT.Copy, [after])
                b = tt(lo[:, k, 0:T], v, hi[:, k, 0:T].bitcast(F), SUB, [a])
            else:
                a = act(hi[:, k, 0:T], v, ACT.Copy, [after], scale=scale)
                b = stt(lo[:, k, 0:T], v, scale, hi[:, k, 0:T].bitcast(F), MUL, SUB, [a])
            return a, b

        class Normed:

            def __init__(self, T, gain, hi=None, lo=None, factor=None, bank=None, hold=True):
                self.T, self.gain, self.hi, self.lo, self.bank = T, gain, hi, lo, STAT if bank is None else bank
                self.factor, self.hold = factor if factor is not None else rstd, hold
                self.tokens, self.held, self.rstd = [None] * KD, [], None
                self.free = None

            def tile(self, k, h, after):
                self.tokens[k] = scaled_parts(k, h, vcol(self.gain, k), self.T, after, None, self.hi, self.lo)
                held = None if (k < NSQ or not self.hold) and not self.held else self.held
                square_sum(h, k, k == 0, k == KD - 1, self.T, after, held, self.bank)

            def finish(self):
                for f in self.held:
                    f()
                self.held = []
                t = sq_free[(KD - 1) % NSQ]
                self.rstd, bank_free[self.bank] = rsqrt_mean(self.factor[:, 0:self.T], banks[self.bank][:, 0:self.T], D,
                                                            [t, last_rstd_use[0]])

        last_rstd_use = [None]

        small = keep("small", [P, 64])
        lb, omlb = small[:, 0:8], small[:, 8:16]
        l0, l1 = vec[:, VEC["lb"]:VEC["lb"] + 8], vec[:, VEC["lb"] + 8:VEC["lb"] + 16]
        t = tt(small[:, 16:24], l0, l1, MAX, [t_vec])
        t1 = tt(small[:, 24:32], l0, small[:, 16:24], SUB, [t])
        t2 = tt(small[:, 32:40], l1, small[:, 16:24], SUB, [t])
        t3 = act(small[:, 24:40], small[:, 24:40], ACT.Exp, [t1, t2])
        t = tt(small[:, 40:48], small[:, 24:32], small[:, 32:40], ADD, [t3])
        t = put("dve", lambda e: e.reciprocal(small[:, 48:56], small[:, 40:48]), [t])
        t = tt(lb, small[:, 24:32], small[:, 48:56], MUL, [t])
        t_lb = ts(omlb, lb, -1.0, MUL, 1.0, ADD, [t])
        nconv = 48 + 12
        conv_half = keep("conv_half", [P, nconv])
        t_half = ts(conv_half[:], vec[:, VEC["m2_conv"]:VEC["m2_conv"] + nconv], 0.5, MUL, after=[t_vec])
        bgate = vec[:, VEC["b_gate"]:VEC["b_gate"] + 24]
        t_bgate = ts(bgate, bgate, 0.5, MUL, after=[t_vec])

        norm1 = Normed(T1, "norm1")
        for k in range(KD):
            norm1.tile(k, H[:, k, :], t_h[k])
        xin = (XH, XL, 0, 0, norm1.tokens)

        phase = top[0]
        cur = [phase]
        O_all = place("O_all", [P, HEADS, T1], F, cur)
        G_all = place("G_all", [P, HEADS, T1], F, cur)
        after_og = cur[0]
        W2 = 2 * T1
        f_, k_, e1, q_ = (place(n, [P, W2], F, cur) for n in ("hg_f", "hg_k", "hg_e", "hg_q"))
        bc = f_
        WP = NCH * WIN
        kinv, kend, v_ = (place(n, [P, 2 * WP], F, cur) for n in ("hg_kinv", "hg_kend", "hg_v"))
        qth = place("hg_tanh", [P, W2], F, cur)
        kx = place("hg_kx", [P, W2], F, cur)
        qdec = [place(f"hg_qdec{i}", [P, W2], F, cur) for i in range(2)]
        decay = [place(f"hg_decay{i}", [P, 2 * NCH], F, cur) for i in range(2)]
        ktok = [place(f"hg_ktok{i}", [P, 4 * P], F, cur) for i in range(2)]
        vtok = [place(f"hg_vtok{i}", [P, 5 * P], F, cur) for i in range(2)]
        score = [place(f"hg_score{i}", [P, T1], F, cur) for i in range(2)]
        state = place("hg_state", [P, NCH - 1, P], F, cur)
        hg_end = cur[0]
        t_pads0 = [memset(t[:], 0.0) for t in (kinv, kend, v_)]
        t_score0 = [memset(score[i][:], 0.0) for i in range(2)]
        cur = [after_og]
        MAH = place("MAH", [P, 8, T1], R, cur)
        MAL = place("MAL", [P, 8, T1], R, cur)
        MBH = place("MBH", [P, 8, T1], R, cur)
        MBL = place("MBL", [P, 8, T1], R, cur)
        Z_ = place("m2_Z", [P, 4, T1], F, cur)
        zth = place("m2_zth", [P, T1], F, cur)
        cur = [max(cur[0], hg_end)]
        PADW = T1 + 3
        npad = 2
        mpad = place("m2_pad", [P, npad, PADW], F, cur)
        mcv = place("m2_cv", [P, 2, T1], F, cur)
        mth = place("m2_th", [P, 2, T1], F, cur)
        BC = place("m2_BC", [P, 4, T1], F, cur)
        CBW = T1 + 144 + 16
        CBT = place("m2_CBT", [P, 2, CBW], F, cur)
        dtT = place("m2_dtT", [P, 3 * M2H], F, cur)
        nacT = place("m2_nacT", [P, 3 * M2H], F, cur)
        DT = [place(f"m2_dt{i}", [M2H, T1], F, cur) for i in range(4)]
        over = [phase]
        SEG = place("m2_SEG", [P, CBW], F, over)
        MT = place("m2_MT", [P, CBW], F, over)
        XTOK = place("m2_XTOK", [P, 3 * P], F, over)
        X_ = place("m2_X", [P, 4, T1], F, over)
        Y_ = place("m2_Y", [P, 4, T1], F, over)
        rg = place("m2_rg", [P, T1], F, over)
        assert over[0] <= after_og
        t_pad = [memset(mpad[:, i, 0:3], 0.0) for i in range(npad)]

        hg = {}

        def pair_slab(col, p, dests, scale=None, name=None, hook=None, free=None):
            def reader(j):
                def read(bank, tok):
                    o = dests[j]
                    extra = free() if free else ()
                    if name == "v":
                        t = tt(o, chunks(bank[:, 0:T1]), chunks(rstd[:]), MUL, [tok, norm1.rstd, t_pads0[2], *extra])
                    elif scale is None:
                        t = tt(o, bank[:, 0:T1], rstd[:], MUL, [tok, norm1.rstd, *extra])
                    else:
                        t = stt(o, bank[:, 0:T1], scale, rstd[:], MUL, MUL, [tok, norm1.rstd, *extra])
                    hg[(name, p, j)] = t
                    last_rstd_use[0] = t
                    return t
                return read
            return Slab(KD, 256, [(0, 256, columns(A["w_in"], col + 256 * p, 256))], xin, T1,
                        [((name, p, 0), 0, P, reader(0)), ((name, p, 1), P, P, reader(1))], hook=hook)

        def halves_of(t):
            return [t[:, 0:T1], t[:, T1:W2]]

        def chunks(t):
            return t.rearrange("p (c s) -> p c s", s=CHUNK)

        def padded(t):
            return t.rearrange("p (c s) -> p c s", s=WIN)[:, :, 0:CHUNK]

        def hg_gates(p):
            prev = hg.get(("prep_done", p - 1))
            tf = [hg[("f", p, j)] for j in range(2)]
            a = act(e1[:], f_[:], ACT.Exp, [*tf, prev], scale=-1.0)
            yield
            b = ts(e1[:], e1[:], 1.0, ADD, after=[a])
            b = put("dve", lambda e: e.reciprocal(k_[:], e1[:]), [b, prev])
            yield
            ln = []
            for j in range(2):
                h = 2 * p + j
                ln.append(ts(f_[:, j * T1:(j + 1) * T1], k_[:, j * T1:(j + 1) * T1], omlb[:, h:h + 1], MUL,
                             lb[:, h:h + 1], ADD, after=[b, t_lb, a]))
            c = ts(k_[:], f_[:], -1.0, MUL, 1.0, ADD, after=ln)
            d = act(f_[:], f_[:], ACT.Ln, [*ln, c])
            yield
            s = put("dve", lambda e: e.tensor_tensor_scan(bc[:], con_("reset", W2), f_[:], 0.0, MUL, ADD),
                    [d, t_con])
            yield
            g = act(e1[:], bc[:], ACT.Exp, [s])
            hg[("eb", p)] = g
            yield
            while ("qa", p) not in hg:
                yield
            th, qt = hg[("qa", p)]
            q = tt(qdec[p % 2][:], q_[:], e1[:], MUL, [g, qt, hg.get(("qdec_free", p - 2))])
            dd = copy(decay[p % 2][:].rearrange("p (c o) -> p c o", o=1), chunks(e1[:])[:, :, CHUNK - 1:CHUNK],
                      [g, hg.get(("qdec_free", p - 2))])
            hg[("q_free", p)] = q
            hg[("qdec", p)] = q
            hg[("decay", p)] = dd
            yield
            i = act(e1[:], bc[:], ACT.Exp, [q, dd], scale=-1.0)
            last = chunks(bc[:])[:, :, CHUNK - 1:CHUNK].to_broadcast([P, 2 * NCH, CHUNK])
            w = tt(chunks(kx[:]), last, chunks(bc[:]), SUB, [s, hg.get(("prep_done", p - 1))])
            hg[("f_free", p)] = (w, i)
            w = act(kx[:], kx[:], ACT.Exp, [w])
            yield
            ki = tt(padded(kinv[:]), chunks(k_[:]), chunks(e1[:]), MUL, [i, c, hg.get(("kinv_free", p - 1)), t_pads0[0]])
            ke = tt(padded(kend[:]), chunks(k_[:]), chunks(kx[:]), MUL, [w, c, hg.get(("kend_free", p - 1)), t_pads0[1]])
            hg[("kinv", p)], hg[("kend", p)] = ki, ke
            hg[("prep_done", p)] = ke
            yield

        def silu_from_half(o, half, scratch, after, extra=()):
            a = act(scratch, half, ACT.Tanh, after)
            return stt(o, scratch, 1.0, half, ADD, MUL, [a, *extra])

        def hg_head(p, j):
            h = 2 * p + j
            sl = slice(j * T1, (j + 1) * T1)
            O = STAT
            head_prev = hg.get(("head_done", p - 1, j))
            base_k, base_v = kend[:, j * WP:(j + 1) * WP], v_[:, j * WP:(j + 1) * WP]

            def tr4(src, dst, after, free, U):
                for T in range(4):
                    tk = transpose(banks[U][:, T * P:(T + 1) * P], src[:, T * P:(T + 1) * P], ident,
                                   [*after, t_con, bank_free[U]] if T == 0 else (), signal=T == 3)
                c = act(dst, banks[U][:, :], ACT.Copy, [tk, free])
                bank_free[U] = c
                return tk, c
            while ("kend", p) not in hg:
                yield
            tk, ck = tr4(base_k, ktok[j][:], [hg[("kend", p)]], head_prev, 3)
            hg[("kend_free", p)] = tk
            yield
            tk, cv = tr4(base_v, vtok[j][:, 0:4 * P], [hg[("v", p, j)]], head_prev, 4)
            yield
            tk = transpose(banks[5][0:CHUNK, 0:P], base_v[:, 4 * P:4 * P + CHUNK], ident, [bank_free[5]], signal=True)
            hg[("v_free", p, j)] = tk
            cv2 = act(vtok[j][0:CHUNK, 4 * P:5 * P], banks[5][0:CHUNK, 0:P], ACT.Copy, [tk])
            bank_free[5] = cv2
            for T in range(5):
                ncol = 64 if T < 4 else CHUNK
                rows = P if T < 4 else CHUNK
                tk = mm(banks[6][0:rows, 64 * T:64 * T + ncol], kinv[:, j * WP + T * P:j * WP + T * P + rows],
                        qdec[p % 2][:, j * T1 + 64 * T:j * T1 + 64 * T + ncol], T == 0, True,
                        [bank_free[6], hg[("kinv", p)], hg[("qdec", p)]] if T == 0 else (), signal=T == 4)
            hg[("kinv_free", p)] = tk
            m1 = put("dve", lambda e: e.copy_predicated(score[j][:, 0:256], chunk_mask[:, 0:256], banks[6][:, 0:256]),
                     [tk, t_mask, t_score0[j], head_prev])
            m2_ = put("dve", lambda e: e.copy_predicated(score[j][0:CHUNK, 256:T1], chunk_mask[0:CHUNK, 256:T1],
                                                         banks[6][0:CHUNK, 256:T1]), [tk])
            bank_free[6] = m2_
            yield
            for T in range(4):
                for c in range(4):
                    rows = slice(32 * c, 32 * c + CHUNK)
                    tk = mm(banks[3 + c][:, T * P:(T + 1) * P], ktok[j][rows, T * P:(T + 1) * P],
                            vtok[j][rows, T * P:(T + 1) * P], T == 0, True,
                            [bank_free[3 + c], ck, cv] if T == 0 else (), signal=T == 3)
                    hg["u", c] = tk
            yield
            upd = None
            ups = {}
            for T in range(6):
                if T >= 1:
                    S = T - 1
                    ncol = 64 if S < 4 else CHUNK
                    rows = P if S < 4 else CHUNK
                    oc = slice(64 * S, 64 * S + ncol)
                    mm(banks[O][:, oc], vtok[j][0:rows, S * P:(S + 1) * P], score[j][0:rows, oc], S == 0, False,
                       [bank_free[O], m1, m2_, cv, cv2] if S == 0 else ())
                    for c in range(4 * S, min(4 * S + 4, NCH)):
                        if c:
                            tk = mm(banks[O][:, c * CHUNK:(c + 1) * CHUNK], state[:, c - 1, :],
                                    qdec[p % 2][:, j * T1 + c * CHUNK:j * T1 + (c + 1) * CHUNK], False, True,
                                    [ups[c - 1]], signal=c % 4 == 3 or c == NCH - 1)
                if T < 4:
                    for c in range(4):
                        n = 4 * T + c
                        u = banks[3 + c][:, T * P:(T + 1) * P]
                        if n == 0:
                            upd = copy(state[:, 0, :], u, [hg["u", c], hg.get("state_free")])
                        else:
                            upd = stt(state[:, n, :], state[:, n - 1, :], decay[p % 2][:, j * NCH + n:j * NCH + n + 1],
                                      u, MUL, ADD, [hg["u", c], upd, hg[("decay", p)]])
                        ups[n] = upd
                        bank_free[3 + c] = upd
                yield
            hg["state_free"] = tk
            hg[("qdec_free", p)] = tk
            hg[("head_done", p, j)] = tk
            c = act(O_all[:, h, :], banks[O][:, 0:T1], ACT.Copy, [tk])
            bank_free[O] = c
            hg[("o", h)] = c

        def hg_norms():
            tl = {}
            prev = [hg[("head_done", 3, j)] for j in range(2)] + [hg[("o", 6)], hg[("o", 7)]]
            for h in range(HEADS):
                t = square_sum(O_all[:, h, :], h, True, True, T1, hg[("o", h)], bank=6)
                a = act(LN8[:, h, :], banks[6][:, 0:T1], ACT.Ln, [t, *prev], scale=1.0 / P, bias=eps)
                bank_free[6] = a
                tl[h] = a
                yield
            for h in range(HEADS):
                a = act(LN8[:, h, :], LN8[:, h, :], ACT.Exp, [tl[h]], scale=-0.5)
                b = stt(O_all[:, h, :], O_all[:, h, :], vcol("hg_norm", h), LN8[:, h, :], MUL, MUL, [a, t_vec])
                c = tt(O_all[:, h, :], O_all[:, h, :], G_all[:, h, :], MUL, [b, hg[("ga", h)]])
                hg[("mix", h)] = parts_of(h, O_all[:, h, :], MAH, MAL, c, T1)
                hg["ln8_free"] = b
                yield

        cur = [after_og + 2 * ((size([P, 8, T1]) + 63) // 64 * 64)]
        LN8 = place("LN8", [P, 8, T1], F, cur)

        hg_slabs = []
        for p in range(4):
            hg_slabs.append((
                pair_slab(C_F, p, halves_of(f_), name="f", free=lambda p=p: hg.get(("f_free", p - 1), ())),
                pair_slab(C_Q, p, halves_of(q_), 0.5, "q", free=lambda p=p: [hg.get(("q_free", p - 1))]),
                pair_slab(C_I, p, [padded(v_[:, j * WP:(j + 1) * WP]) for j in range(2)], name="v",
                          free=lambda p=p: [hg.get(("v_free", p - 1, 0)), hg.get(("v_free", p - 1, 1))]),
                pair_slab(C_G, p, [G_all[:, 2 * p + j, :] for j in range(2)], 0.5, "g")))
        hg_slabs[0][0].hook = norm1.finish

        m2 = {}
        tap_free = {}

        def conv_tile(m, T, K, pad, cv, w, b, after, taps_free=None):
            first = pad[:, K - 1:K - 1 + T]
            if b is None:
                t = act(cv, first, ACT.Copy, [*after, taps_free], scale=w(K - 1))
            else:
                t = act(cv, first, ACT.Identity, [*after, taps_free], scale=w(K - 1), bias=b)
            for k in range(K - 1):
                t = stt(cv, pad[:, k:k + T], w(k), cv, MUL, ADD, [t])
            return t

        pad_turn = [0]
        pad_free = [None] * npad

        def xbc_reader(m, dest, dest_free):
            def read(bank, tok):
                i = pad_turn[0] % npad
                pad_turn[0] += 1
                t = tt(mpad[:, i, 3:3 + T1], bank[:, 0:T1], rstd[:], MUL, [tok, norm1.rstd, pad_free[i], t_pad[i]])
                last_rstd_use[0] = t
                c = conv_tile(m, T1, 4, mpad[:, i, :], mcv[:, i, :],
                              lambda k: conv_half[:, 12 * k + m:12 * k + m + 1], conv_half[:, 48 + m:49 + m],
                              [t, t_half, pad_free[i]])
                r = silu_from_half(dest, mcv[:, i, :], mth[:, i, :], [c], [dest_free()])
                pad_free[i] = r
                m2[("xbc", m)] = r
                return t
            return read

        def dt_reader(bank, tok):
            t = tt(DT[0][:], bank[0:M2H, 0:T1], rstd[0:M2H, :], MUL, [tok, norm1.rstd])
            last_rstd_use[0] = t
            m2["dt_raw"] = t
            return t

        def m2_steps():
            x, e, s, d = DT
            t = ts(x[:], x[:], heads16[:, 0:1], ADD, after=[m2["dt_raw"], t_hd])
            a = act(e[:], x[:], ACT.Abs, [t])
            a = act(e[:], e[:], ACT.Exp, [a], scale=-1.0)
            yield
            b = ts(s[:], e[:], 2.0, ADD, after=[a])
            b = put("dve", lambda e_: e_.reciprocal(s[:], s[:]), [b])
            b = tt(s[:], s[:], e[:], MUL, [b])
            yield
            c = tt(e[:], s[:], s[:], MUL, [b])
            terms = 9
            c = ts(d[:], e[:], 2.0 / (2 * terms + 1), MUL, after=[c])
            for n in range(terms - 1, 0, -1):
                c = stt(d[:], d[:], 2.0 / (2 * n + 1), e[:], ADD, MUL, [c])
                if n % 3 == 0:
                    yield
            c = stt(d[:], d[:], 2.0, s[:], ADD, MUL, [c])
            c = stt(d[:], x[:], 0.0, d[:], MAX, ADD, [c])
            z = act(heads16[:, 2:3], heads16[:, 1:2], ACT.Exp, [t_hd])
            z = ts(heads16[:, 3:4], heads16[:, 2:3], -1.0, MUL, after=[z])
            z = ts(x[:], d[:], heads16[:, 3:4], MUL, after=[z, c])
            yield
            z = put("dve", lambda e_: e_.tensor_tensor_scan(e[:], con_("ones", T1, M2H), x[:], 0.0, MUL, ADD), [z, t_con])
            m2["acum"] = z
            n = None
            for i, (src, tok) in enumerate(((d, c), (e, z))):
                for jt in range(3):
                    rows = P if jt < 2 else 16
                    n = transpose(banks[STAT][0:rows, 48 * i + 16 * jt:48 * i + 16 * jt + 16],
                                  src[:, jt * P:jt * P + rows], con_("ident", M2H, M2H), [tok, bank_free[STAT]],
                                  signal=True)
            yield
            r = None
            for c0, rows in ((0, P), (32, 16)):
                w = 32 if c0 == 0 else 16
                r = ts(dtT[0:rows, c0:c0 + w], banks[STAT][0:rows, c0:c0 + w], 1.0, MUL, after=[n])
                r = ts(nacT[0:rows, c0:c0 + w], banks[STAT][0:rows, 48 + c0:48 + c0 + w], -1.0, MUL, after=[n])
            bank_free[STAT] = r
            m2["rows"] = r
            yield
            for g in range(2):
                Bt, Ct = BC[:, g, :], BC[:, 2 + g, :]
                for jt, (c0, w, rows) in enumerate(BLOCKS):
                    n = mm(banks[STAT][0:rows, c0:c0 + w], Bt[:, jt * P:jt * P + rows], Ct[:, jt * P:jt * P + w],
                           jt == 0, True, [m2[("xbc", 8 + g)], m2[("xbc", 10 + g)], bank_free[STAT]], signal=jt == 2)
                q1 = copy(CBT[:, g, 0:416], banks[STAT][:, 0:416], [n])
                q2 = copy(CBT[0:16, g, 416:432], banks[STAT][0:16, 416:432], [n])
                bank_free[STAT] = q2
                for jt, (c0, w, rows) in enumerate(BLOCKS):
                    dg = CBT[0:rows, g, c0:c0 + rows]
                    r = put("pool", lambda e_, dg=dg, rows=rows: e_.affine_select(
                        out=dg, in_=dg, compare_op=ALU.is_ge, fill=0.0, base=0, pattern=[[1, rows]],
                        channel_multiplier=-1), [q1, q2])
                m2[("cbt", g)] = r
                yield

        BLOCKS = [(0, T1, P), (T1, T1 - P, P), (2 * T1 - P, T1 - 2 * P, T1 - 2 * P)]

        def m2_tile(m):
            g = m // 4
            X, Z, Y = X_[:, m % 4, :], Z_[:, m % 4, :], Y_[:, m % 4, :]
            TR, BB, YB = 3, 4, 5
            while ("xbc", m) not in m2 or ("cbt", g) not in m2 or ("z", m) not in m2:
                yield
            tx = m2[("xbc", m)]
            for jt, (c0, w, rows) in enumerate(BLOCKS):
                n = transpose(banks[TR][0:rows, jt * P:(jt + 1) * P], X[:, jt * P:jt * P + rows], ident,
                              [tx, bank_free[TR]], signal=True)
            c1 = act(XTOK[:, 0:2 * P], banks[TR][:, 0:2 * P], ACT.Copy, [n, m2.get("xtok_free")])
            c2 = act(XTOK[0:16, 2 * P:3 * P], banks[TR][0:16, 2 * P:3 * P], ACT.Copy, [n])
            bank_free[TR] = c2
            yield
            for e in range(2):
                h = 2 * m + e
                n = mm(banks[BB][:, 0:T1], con_("ident", M2H, M2H)[:, h:h + 1].to_broadcast([M2H, P]), DT[1][:],
                       True, True, [m2["acum"], bank_free[BB]], signal=True)
                for jt, (c0, w, rows) in enumerate(BLOCKS):
                    s = ts(SEG[0:rows, c0:c0 + w], banks[BB][0:rows, jt * P:T1], nacT[0:rows, 16 * jt + h:16 * jt + h + 1],
                           ADD, 0.0, MIN, after=[n, m2["rows"], m2.get("seg_free")])
                bank_free[BB] = s
                yield
                a = act(SEG[:, 0:416], SEG[:, 0:416], ACT.Exp, [s])
                a = act(SEG[0:16, 416:432], SEG[0:16, 416:432], ACT.Exp, [s])
                for jt, (c0, w, rows) in enumerate(BLOCKS):
                    s = stt(MT[0:rows, c0:c0 + w], SEG[0:rows, c0:c0 + w], dtT[0:rows, 16 * jt + h:16 * jt + h + 1],
                            CBT[0:rows, g, c0:c0 + w], MUL, MUL, [a, m2["rows"], m2[("cbt", g)], m2.get("mt_free")])
                m2["seg_free"] = s
                yield
                for jt, (c0, w, rows) in enumerate(BLOCKS):
                    n = mm(banks[YB][64 * e:64 * e + 64, jt * P:T1], XTOK[0:rows, jt * P + 64 * e:jt * P + 64 * e + 64],
                           MT[0:rows, c0:c0 + w], jt == 0, jt == 2, [s, c1, c2, bank_free[YB]], signal=jt == 2)
                m2["mt_free"] = n
                m2["xtok_free"] = n
            yield
            y = stt(Y, X, vcol("m2_d", m), banks[YB][:, 0:T1], MUL, ADD, [n, t_vec, tx, m2.get(("y_free", m - 4))])
            bank_free[YB] = y
            m2[("x_free", m)] = y
            y = tt(Y, Y, Z, MUL, [y, m2[("z", m)]])
            m2[("z_free", m)] = y
            t = square_sum(Y, m, m % 4 == 0, m % 4 == 3, T1, y)
            yield
            if m % 4 == 3:
                r, bank_free[STAT] = rsqrt_mean(rg[:], banks[STAT][:, 0:T1], 4 * P, [t, m2.get("rg_free")])
                for i in range(4):
                    k = 4 * g + i
                    b = stt(Y_[:, i, :], Y_[:, i, :], vcol("m2_norm", k), rg[:], MUL, MUL, [r, y])
                    m2[("mix", k)] = parts_of(k, Y_[:, i, :], MBH, MBL, b, T1)
                    m2[("y_free", k)] = m2[("mix", k)][1]
                    yield
                m2["rg_free"] = b
            m2[("tile_done", m)] = True

        def z_reader(m):
            def read(bank, tok):
                Z = Z_[:, m % 4, :]
                t = stt(Z, bank[:, 0:T1], 0.5, rstd[:], MUL, MUL, [tok, norm1.rstd, m2.get(("z_free", m - 4))])
                last_rstd_use[0] = t
                i = pad_turn[0] % 2
                m2[("z", m)] = silu_from_half(Z, Z, zth[:], [t, m2.get("zth_free")])
                m2["zth_free"] = m2[("z", m)]
                return t
            return read
        def slab2(w, col, readers, key, x, T, hook=None, nk=KD, k0=0, first=True, last=True, wk0=0):
            return Slab(nk, P * len(readers), [(0, P * len(readers), columns(w, col, P * len(readers), wk0, nk))],
                        x, T, [((key, i), P * i, P, r) for i, r in enumerate(readers)], first, last, hook)

        none = lambda: None
        dt_slab = Slab(KD, M2H, [(0, M2H, columns(A["w_in"], C_DT, M2H))], xin, T1, [("dt", 0, M2H, dt_reader)])
        b_slab = slab2(A["w_in"], C_B, [xbc_reader(8 + i, BC[:, i, :], none) for i in range(2)], "B", xin, T1)
        c_slab = slab2(A["w_in"], C_C, [xbc_reader(10 + i, BC[:, 2 + i, :], none) for i in range(2)], "C", xin, T1)
        m2_slabs = []
        for q in range(4):
            m2_slabs.append((
                slab2(A["w_in"], C_Z + 256 * q, [z_reader(2 * q + i) for i in range(2)], ("z", q), xin, T1),
                slab2(A["w_in"], C_X + 256 * q, [xbc_reader(2 * q + i, X_[:, (2 * q + i) % 4, :],
                      lambda m=2 * q + i: m2.get(("x_free", m - 4))) for i in range(2)], ("x", q), xin, T1)))

        wo = {}
        norm2 = Normed(T1, "norm2")

        def add_reader(m, nxt):
            def read(bank, tok):
                t = tt(H[:, m, :], bank[:, 0:T1], H[:, m, :], ADD, [tok, wo.get(m)])
                wo[m] = t
                if nxt is not None:
                    nxt.tile(m, H[:, m, :], t)
                return t
            return read
        mixA = [None] * 8
        mixB = [None] * 8
        outA = [slab2(A["w_out"], 256 * q, [add_reader(2 * q + i, None) for i in range(2)], ("oa", q),
                      (MAH, MAL, 0, 0, mixA), T1) for q in range(4)]
        outB = [slab2(A["w_out"], 256 * q, [add_reader(2 * q + i, norm2) for i in range(2)], ("ob", q),
                      (MBH, MBL, 0, 0, mixB), T1, wk0=8) for q in range(4)]

        def ffn(tag, T, w_up, w_down, conv, conv_b, norm, x, down_reader, mem):
            AH, AL = mem["AH"], mem["AL"]
            acts = [None] * MF
            pad, cv, sg, av = mem["pad"], mem["cv"], mem["sg"], mem["av"]
            NP = 4
            pfree, cfree, afree = [None] * NP, [None] * NP, [None] * 2
            turnp = [0]
            f = {}

            def reader(m, is_val):
                def read(bank, tok):
                    i = turnp[0] % NP
                    turnp[0] += 1
                    t = tt(pad[:, i, 2:2 + T], bank[:, 0:T], rstd[:, 0:T], MUL, [tok, norm.rstd, pfree[i], mem["t_pad"][i]])
                    last_rstd_use[0] = t
                    mm_ = m + MF * is_val
                    c = conv_tile(m, T, 3, pad[:, i, :], cv[:, i, 0:T], lambda k: vcol(conv, 44 * k + mm_),
                                  vcol(conv_b, mm_) if conv_b else None, [t, cfree[i], mem["start"]])
                    pfree[i] = c
                    if not is_val:
                        s = act(sg[:, m % 2, 0:T], cv[:, i, 0:T], ACT.Silu, [c, f.get(("sg", m - 2)), mem["start"]])
                        cfree[i] = s
                        f[("gate", m)] = s
                    else:
                        j = m % 2
                        s = tt(av[:, j, 0:T], sg[:, m % 2, 0:T], cv[:, i, 0:T], MUL, [c, f[("gate", m)], afree[j], mem["start"]])
                        cfree[i] = s
                        f[("sg", m)] = s
                        acts[m] = parts_of(m, av[:, j, 0:T], AH, AL, s, T)
                        afree[j] = acts[m][1]
                    return t
                return read
            ups, downs = [], []
            for q in range(MF // 2):
                ups.append(slab2(w_up, 256 * q, [reader(2 * q + i, 0) for i in range(2)], (tag, "g", q), x, T))
                ups.append(slab2(w_up, FF + 256 * q, [reader(2 * q + i, 1) for i in range(2)], (tag, "v", q), x, T))
            for q in range(4):
                for k0, nk in ((0, 8), (8, 8), (16, 6)):
                    downs.append(slab2(w_down, 256 * q, [down_reader(2 * q + i) for i in range(2)], (tag, "d", q),
                                       (AH, AL, k0, 0, acts), T, nk=nk, wk0=k0, first=k0 == 0, last=k0 == 16))
            return ups, downs

        cur = [phase]
        ffn_mem = {"AH": place("AH", [P, MF, T1], R, cur), "AL": place("AL", [P, MF, T1], R, cur),
                   "pad": place("ff_pad", [P, 4, T1 + 2], F, cur), "cv": place("ff_cv", [P, 4, T1], F, cur),
                   "sg": place("ff_sg", [P, 2, T1], F, cur), "av": place("ff_av", [P, 2, T1], F, cur)}
        ffn_end = cur[0]

        class Sums:

            def __init__(self, T):
                self.T, self.held, self.tokens = T, [], [None] * KD

            def tile(self, k, h, after):
                self.tokens[k] = after
                square_sum(h, k, k == 0, k == KD - 1, self.T, after, None if k < NSQ else self.held)

        Sums.finish = Normed.finish
        norm_f = Sums(T1)
        norm_f.factor, norm_f.bank = rstd, STAT

        def down1_reader(m):
            def read(bank, tok):
                t = tt(H[:, m, :], bank[:, 0:T1], H[:, m, :], ADD, [tok])
                norm_f.tile(m, H[:, m, :], t)
                return t
            return read
        up1, down1 = ffn("f1", T1, A["ffn_w_up"], A["ffn_w_down"], "f1_conv", "f1_conv_b", norm2,
                         (XH, XL, 0, 0, norm2.tokens), down1_reader, ffn_mem)


        H2 = [H[:, k, META:T1] for k in range(KD)]
        cur = [ffn_end]
        MEMR = place("MEMR", [P, KD, T2], F, cur)
        MEMH = place("MEMH", [P, KD, T2], R, cur)
        MEML = place("MEML", [P, KD, T2], R, cur)
        mem_rstd = place("mem_rstd", [P, T2], F, cur)
        norm_m = Normed(T2, "g_mem", MEMH, MEML, mem_rstd, bank=6, hold=False)
        norm_g = Normed(T2, "g_mix", bank=6)
        norm_h = Normed(T2, "g_ffn")
        xin2 = (XH, XL, 0, 0, norm_g.tokens)
        NB = T2 // P

        cur = [phase]
        con2 = place("con2", [P, NCON - NCON1], F, cur)
        con2_ = lambda name, w: con2[:, CON[name] - NCON1:CON[name] - NCON1 + w]
        kmT = place("kmT", [P, 2, T2], F, cur)
        vmtok = place("vmtok", [P, NB, 2 * P], F, cur)
        rraw = place("rraw", [P, 2, T2], F, cur)
        qiT = place("qiT", [P, 2, T2], F, cur)
        kiT = place("kiT", [P, T2], F, cur)
        qT = place("qT", [P, 3, T2], F, cur)
        kT = place("kT", [P, T2], F, cur)
        vT = place("vT", [P, 2, T2], F, cur)
        vtok2 = place("vtok", [P, NB, P], F, cur)
        wi = place("wi", [IDX_HEADS, T2], F, cur)
        wiT = place("wiT", [P, NB * IDX_HEADS], F, cur)
        relu = place("relu", [P, 4, T2], F, cur)
        sco = place("sco", [P, 2, T2], F, cur)
        pen = place("pen", [P, 2, T2], F, cur)
        max8 = place("max8", [P, 8], F, cur)
        soft = place("soft", [P, 4, 4], F, cur)
        qcT = place("qcT", [P, 2, T2], F, cur)
        prob = relu
        PT = place("PT", [P, 2, 4 * P], F, cur)
        CG = place("CG", [P, 3, T2], F, cur)
        cpad = place("cpad", [P, T2 + 2], F, cur)
        ccv = place("ccv", [P, 3, T2], F, cur)
        ctmp = place("ctmp", [P, T2], F, cur)
        temps_end = cur[0]
        YAH, YAL = place("YAH", [P, 3, T2], R, cur), place("YAL", [P, 3, T2], R, cur)
        YCH, YCL = place("YCH", [P, 3, T2], R, cur), place("YCL", [P, 3, T2], R, cur)
        YMH, YML = place("YMH", [P, 2, T2], R, cur), place("YML", [P, 2, T2], R, cur)
        G2 = place("G2", [P, 24, T2], F, cur)
        cur = [phase]
        MG = place("MG", [P, KD, T2], F, cur)
        MGH, MGL = place("MGH", [P, KD, T2], R, cur), place("MGL", [P, KD, T2], R, cur)
        mtmp = place("mtmp", [P, 2, T2], F, cur)
        assert cur[0] <= temps_end
        b2 = {}

        def scaled(o, bank, tok, norm=None, extra=()):
            norm = norm or norm_g
            t = tt(o, bank[0:o.shape[0], 0:T2], norm.factor[0:o.shape[0], 0:T2], MUL, [tok, norm.rstd, *extra])
            if norm is norm_g:
                last_rstd_use[0] = t
            return t

        def plain(name, o, norm=None):
            def read(bank, tok):
                b2[name] = scaled(o, bank, tok, norm)
                return b2[name]
            return read

        rope_turn = [0]
        rope_free = [None] * 2

        def roped(name, o, rot, cos, sin):
            def read(bank, tok):
                i = rope_turn[0] % 2
                rope_turn[0] += 1
                t = scaled(rraw[:, i, :], bank, tok, extra=[rope_free[i]])
                n = mm(banks[STAT][:, 0:T2], con2_(rot, P), rraw[:, i, :], True, True,
                       [t, t_con2[0], bank_free[STAT]], signal=True)
                rope_free[i] = n
                r = {}

                def rest():
                    a = tt(o, rraw[:, i, :], con2_(cos, T2), MUL, [t, t_con2[0]])
                    b = tt(ctmp[:], banks[STAT][:, 0:T2], con2_(sin, T2), MUL, [n, b2.get("ctmp_free")])
                    bank_free[STAT] = b
                    b2[name] = tt(o, o, ctmp[:], ADD, [a, b])
                    b2["ctmp_free"] = b2[name]
                    rope_free[i] = a
                rest()
                return t
            return read

        t_con2 = [None]

        def wi_reader(bank, tok):
            t = scaled(wi[:], bank, tok)
            for n in range(NB):
                r = transpose(banks[STAT][:, n * IDX_HEADS:(n + 1) * IDX_HEADS], wi[:, n * P:(n + 1) * P],
                              con_("ident", IDX_HEADS, IDX_HEADS), [t, bank_free[STAT]], signal=True)
            b2["wi"] = ts(wiT[:], banks[STAT][:, 0:NB * IDX_HEADS], (IDX_HEADS * 32) ** -0.5, MUL, after=[r])
            bank_free[STAT] = b2["wi"]
            return t

        def token_major(name, src, dst, width, after):
            for n in range(NB):
                for c in range(width // P):
                    r = transpose(banks[STAT][:, (n * (width // P) + c) * P:(n * (width // P) + c + 1) * P],
                                  src[:, c, n * P:(n + 1) * P], ident, [after, bank_free[STAT]], signal=True)
            b2[name] = act(dst, banks[STAT][:, 0:NB * width], ACT.Copy, [r])
            bank_free[STAT] = b2[name]

        def vm_reader(i):
            def read(bank, tok):
                t = scaled(vT[:, i, :], bank, tok, norm_m)
                if i == 1:
                    token_major("vmtok", vT, vmtok[:].rearrange("p n c -> p (n c)"), 2 * P, t)
                return t
            return read

        def v_reader(bank, tok):
            t = scaled(vT[:, 0, :], bank, tok, extra=[b2["vmtok"]])
            token_major("vtok", vT, vtok2[:].rearrange("p n c -> p (n c)"), P, t)
            return t

        def cg_reader(i):
            return plain(("cg", i), CG[:, i, :])

        def u_reader(i):
            def read(bank, tok):
                t = scaled(ctmp[:], bank, tok, extra=[b2.get("ctmp_free")])
                r = tt(cpad[:, 2:], ctmp[:], CG[:, i, :], MUL, [t, b2[("cg", i)], b2.get("cpad_free"), b2["cpad0"]])
                b2["ctmp_free"] = r
                r = conv_tile(i, T2, 3, cpad[:], ccv[:, i, :], lambda k: vcol("short", 3 * k + i), None, [r])
                b2["cpad_free"] = b2[("ccv", i)] = r
                return t
            return read

        def bg_reader(i):
            def read(bank, tok):
                t = scaled(ctmp[:], bank, tok, extra=[b2.get("ctmp_free")])
                r = tt(ccv[:, i, :], ccv[:, i, :], ctmp[:], MUL, [t, b2[("ccv", i)]])
                b2["ctmp_free"] = r
                b2[("yc", i)] = parts_of(i, ccv[:, i, :], YCH, YCL, r, T2)
                return t
            return read

        def gate_reader(m):
            def read(bank, tok):
                t = scaled(G2[:, m, :], bank, tok)
                b2[("gate", m)] = act(G2[:, m, :], G2[:, m, :], ACT.Tanh, [t, t_bgate], scale=0.5,
                                      bias=vcol("b_gate", m))
                return t
            return read

        def wcols(col, n):
            return columns(A["w_in_2"], col, n)

        def pairs(*tiles):
            c0, pieces, parts = 0, [], []
            for key, cols, M, reader in tiles:
                for off, w, col in cols:
                    pieces.append((c0 + off, w, wcols(col, w)))
                parts.append((key, c0, M, reader))
                c0 += M
            return Slab(KD, c0, pieces, xin2, T2, parts)

        def q_tile(r):
            return (("q", r), [(0, 64, C2_Q + 64 * r), (64, 64, C2_Q + 64 * (3 + r))], P,
                    roped(("q", r), qT[:, r, :], "rot_a", "cos_a", "sin_a"))

        def tile_(key, col, reader):
            return (key, [(0, P, col)], P, reader)

        xm = (MEMH, MEML, 0, 0, norm_m.tokens)
        mem_slabs = [slab2(A["w_mem_kv_2"], 0, [plain(("km", i), kmT[:, i, :], norm_m) for i in range(2)], "km", xm, T2),
                     slab2(A["w_mem_kv_2"], 256, [vm_reader(i) for i in range(2)], "vm", xm, T2)]
        in2 = [
            pairs(*[tile_(("qi", t), C2_QI + P * t, roped(("qi", t), qiT[:, t, :], "rot_i", "cos_i", "sin_i"))
                    for t in range(2)]),
            pairs(("ki", [(32 * i, 32, C2_KI) for i in range(4)], P, roped("ki", kiT[:], "rot_i", "cos_i", "sin_i")),
                  ("wi", [(0, IDX_HEADS, C2_WI)], IDX_HEADS, wi_reader)),
            pairs(q_tile(0), q_tile(1)),
            pairs(q_tile(2), tile_("k", C2_K, roped("k", kT[:], "rot_a", "cos_a", "sin_a"))),
            pairs(tile_("v", C2_V, v_reader), tile_("cg0", C2_CG, cg_reader(0))),
            pairs(*[tile_(("qc", t), C2_QC + P * t, plain(("qc", t), qcT[:, t, :])) for t in range(2)]),
            pairs(tile_("u0", C2_U, u_reader(0)), tile_("cg1", C2_CG + P, cg_reader(1))),
            pairs(tile_("u1", C2_U + P, u_reader(1)), tile_("cg2", C2_CG + 2 * P, cg_reader(2))),
            pairs(tile_("u2", C2_U + 2 * P, u_reader(2)), tile_("bg0", C2_BG, bg_reader(0))),
            pairs(tile_("bg1", C2_BG + P, bg_reader(1)), tile_("bg2", C2_BG + 2 * P, bg_reader(2))),
        ] + [pairs(*[tile_(("gate", m), C2_GATE + P * m, gate_reader(m)) for m in (2 * q, 2 * q + 1)]) for q in range(12)]

        def merge_reader(branch, m):
            def read(bank, tok):
                g = G2[:, branch * KD + m, :]
                if branch == 0:
                    t = stt(MG[:, m, :], g, 1.0, bank[:, 0:T2], ADD, MUL, [tok, b2[("gate", m)]])
                    b2[("mg", m)] = t
                    return t
                i = m % 2
                t = stt(mtmp[:, i, :], g, 1.0, bank[:, 0:T2], ADD, MUL, [tok, b2[("gate", branch * KD + m)], b2.get(("mtmp", i))])
                r = tt(MG[:, m, :], MG[:, m, :], mtmp[:, i, :], ADD, [t, b2[("mg", m)]])
                b2[("mtmp", i)] = b2[("mg", m)] = r
                if branch == 2:
                    merged[m] = parts_of(m, MG[:, m, :], MGH, MGL, r, T2, scale=0.5)
                return t
            return read

        merged, ya, yc, ym = [None] * KD, [None] * 3, [None] * 3, [None] * 2
        out2 = []
        for half in range(2):
            c, ms = 512 * half, range(4 * half, 4 * half + 4)
            att = A["w_att_out_2"].rearrange("(g r p) n -> g p r n", g=2, r=3)
            out2.append(Slab(3, 512, [(0, 512, att[g, :, :, c:c + 512], 64 * g, 64 * g + 64) for g in range(2)],
                             (YAH, YAL, 0, 0, ya), T2, [(("at", m), P * (m % 4), P, merge_reader(0, m)) for m in ms]))
            out2.append(Slab(3, 512, [(0, 512, columns(A["w_conv_out_2"], c, 512, 0, 3))],
                             (YCH, YCL, 0, 0, yc), T2, [(("co", m), P * (m % 4), P, merge_reader(1, m)) for m in ms]))
            out2.append(Slab(2, 512, [(0, 512, columns(A["w_mem_out_2"], c, 512, 0, 2))],
                             (YMH, YML, 0, 0, ym), T2, [(("me", m), P * (m % 4), P, merge_reader(2, m)) for m in ms]))

        def add2_reader(m, nxt):
            def read(bank, tok):
                t = tt(H2[m], bank[:, 0:T2], H2[m], ADD, [tok])
                nxt.tile(m, H2[m], t)
                return t
            return read
        wo2 = [slab2(A["w_o_2"], 256 * q, [add2_reader(2 * q + i, norm_h) for i in range(2)], ("wo2", q),
                     (MGH, MGL, 0, 0, merged), T2) for q in range(4)]
        norm_o = Sums(T2)
        norm_o.factor, norm_o.bank = rstd, STAT
        ffn_mem2 = dict(ffn_mem)
        up2, down2 = ffn("f2", T2, A["w_up_2"], A["w_down_2"], "f2_conv", None, norm_h,
                         (XH, XL, 0, 0, norm_h.tokens), lambda m: add2_reader(m, norm_o), ffn_mem2)

        def attend(qs, ks, vals, r, penalty, hi, lo, key):
            for e in range(2):
                half = slice(64 * e, 64 * e + 64)
                pt = PT[:, e, :]
                for n in range(NB):
                    S = (n + 1) * P if penalty else T2
                    i = 2 * e + n
                    pr = prob[:, i, 0:S]
                    mx, nm, sm, rc = (soft[:, i, c:c + 1] for c in range(4))
                    lg = banks[3 + e][:, 0:S]
                    t = mm(lg, qs[half, n * P:(n + 1) * P], ks[half, 0:S], True, True,
                           [bank_free[3 + e], *key], signal=True)
                    if penalty:
                        a = put("dve", lambda e_, pr=pr, lg=lg, mx=mx, n=n, S=S: e_.tensor_tensor_reduce(
                            pr, lg, pen[:, n, 0:S], 1.0, -3.0e38, ADD, MAX, mx), [t, b2[("pen", n)], b2.get(("prob", i))])
                        bank_free[3 + e] = a
                        src = pr
                    else:
                        a = put("dve", lambda e_, lg=lg, mx=mx: e_.reduce_max(mx, lg, AX.X), [t, b2.get(("prob", i))])
                        src = lg
                    a = ts(nm, mx, -(64 ** -0.5), MUL, after=[a])
                    a = act(pr, src, ACT.Exp, [a, b2.get(("prob", i))], scale=64 ** -0.5, bias=nm, accum=sm)
                    if not penalty:
                        bank_free[3 + e] = a
                    yield
                    a = put("dve", lambda e_, rc=rc, sm=sm: e_.reciprocal(rc, sm), [a])
                    a = ts(pr, pr, rc, MUL, after=[a])
                    for b in range(S // P):
                        col = b * T2 + n * P if not (penalty and b) else T2
                        t = transpose(banks[5][:, col:col + P], prob[:, i, b * P:(b + 1) * P], ident,
                                      [a, bank_free[5]], signal=True)
                    b2[("prob", i)] = t
                w = 3 * P if penalty else 4 * P
                c = act(pt[:, 0:w], banks[5][:, 0:w], ACT.Copy, [t, b2.get(("pt", e))])
                bank_free[5] = c
                yield
                vcols = slice(64 * e, 64 * e + 64)
                mm(banks[6][half, 0:T2], vals[:, 0, vcols], pt[:, 0:T2], True, False, [c, bank_free[6], b2["vtok"]])
                if penalty:
                    t = mm(banks[6][half, P:T2], vals[:, 1, vcols], pt[:, T2:T2 + P], False, True, signal=True)
                else:
                    t = mm(banks[6][half, 0:T2], vals[:, 1, vcols], pt[:, T2:2 * T2], False, True, signal=True)
                b2[("pt", e)] = t
            o = parts_of(r, banks[6][:, 0:T2], hi, lo, t, T2)
            bank_free[6] = o[1]
            return o

        def attention():
            while "wi" not in b2 or "ki" not in b2 or ("qi", 1) not in b2:
                yield
            for n in range(NB):
                S = (n + 1) * P
                acc = None
                for t_ in range(2):
                    for h in range(4):
                        rows = slice(32 * h, 32 * h + 32)
                        t = mm(banks[3 + h][:, 0:S], qiT[rows, t_, n * P:(n + 1) * P], kiT[rows, 0:S], True, True,
                               [b2[("qi", t_)], b2["ki"], bank_free[3 + h]], signal=True)
                        a = act(relu[:, h, 0:S], banks[3 + h][:, 0:S], ACT.Relu, [t, b2.get(("relu", h))])
                        bank_free[3 + h] = a
                        w = wiT[:, n * IDX_HEADS + 4 * t_ + h:n * IDX_HEADS + 4 * t_ + h + 1]
                        if acc is None:
                            acc = ts(sco[:, n, 0:S], relu[:, h, 0:S], w, MUL, after=[a, b2["wi"]])
                        else:
                            acc = stt(sco[:, n, 0:S], relu[:, h, 0:S], w, sco[:, n, 0:S], MUL, ADD, [a, acc])
                        b2[("relu", h)] = acc
                        if h % 2:
                            yield
                dg = sco[:, n, n * P:S]
                acc = put("pool", lambda e, dg=dg: e.affine_select(out=dg, in_=dg, compare_op=ALU.is_ge, fill=FILL, base=0,
                                                                   pattern=[[-1, P]], channel_multiplier=1), [acc])
                b2[("sco", n)] = acc
            for n in range(NB):
                S = (n + 1) * P
                a = b2[("sco", n)]
                s_ = sco[:, n, 0:S]
                for r in range(TOPK // 8):
                    a = put("dve", lambda e, s_=s_: e.max(max8[:], s_), [a])
                    a = put("dve", lambda e, s_=s_: e.match_replace(s_, max8[:], s_, TAKEN), [a])
                    if r % 2:
                        yield
                a = ts(pen[:, n, 0:S], s_, TAKEN, ALU.not_equal, PENALTY, MUL, after=[a])
                dg = pen[:, n, n * P:S]
                b2[("pen", n)] = put("pool", lambda e, dg=dg: e.affine_select(
                    out=dg, in_=dg, compare_op=ALU.is_ge, fill=PENALTY, base=0, pattern=[[-1, P]],
                    channel_multiplier=1), [a])
            while "k" not in b2 or "vtok" not in b2:
                yield
            for r in range(3):
                ya[r] = yield from attend(qT[:, r, :], kT[:], vtok2, r, True, YAH, YAL, [b2["k"], b2[("q", r)]])
            while ("qc", 1) not in b2:
                yield
            for r in range(2):
                ym[r] = yield from attend(qcT[:, r, :], kmT[:, r, :], vmtok[:, :, r * P:(r + 1) * P], r, False, YMH, YML,
                                          [b2[("km", r)], b2[("qc", r)], b2["vmtok"]])

        def start2():
            norm_f.finish()
            t = None
            for k in range(KD):
                t = stt(H2[k], H2[k], vcol("final1", k), rstd[:, META:T1], MUL, MUL, [norm_f.rstd, t_vec])
                last_rstd_use[0] = t
                norm_g.tile(k, H2[k], t)
        gens = {}
        for p in range(4):
            sf, sq_, si, sg_ = hg_slabs[p]
            run(sf, 2)
            gates = hg_gates(p)
            background.append(gates)
            run(sq_)
            def q_silu(p=p):
                a = act(qth[:], q_[:], ACT.Tanh, [hg[("q", p, 0)], hg[("q", p, 1)], hg.get("qth_free")])
                b = stt(q_[:], qth[:], 1.0, q_[:], ADD, MUL, [a])
                hg["qth_free"] = b
                hg[("qa", p)] = (a, b)
            q_silu()
            run(si)
            finish(gates)
            if p:
                finish(*gens[p - 1])
            def pair_of(p):
                for j in range(2):
                    yield from hg_head(p, j)
            gens[p] = [pair_of(p)]
            background.extend(gens[p])
            run(sg_, 2)
            for j in range(2):
                h = 2 * p + j
                a = act(qth[:, 0:T1], G_all[:, h, :], ACT.Tanh, [hg[("g", p, j)], hg.get("qth_free")])
                hg[("ga", h)] = stt(G_all[:, h, :], qth[:, 0:T1], 1.0, G_all[:, h, :], ADD, MUL, [a])
                hg["qth_free"] = hg[("ga", h)]
        run(dt_slab)
        m2_gen = m2_steps()
        run(b_slab)
        run(c_slab)
        finish(*gens[3])
        background.append(m2_gen)
        norms = hg_norms()
        background.append(norms)

        def m2_tiles():
            for m in range(8):
                yield from m2_tile(m)
        tiles = m2_tiles()
        for q in range(4):
            while q >= 2 and ("tile_done", 2 * q - 3) not in m2:
                advance()
            run(m2_slabs[q][0], 2)
            if q == 0:
                finish(m2_gen, norms)
                background.append(tiles)
            run(m2_slabs[q][1], 2)
        for k in range(8):
            mixA[k] = hg[("mix", k)]
        for s in outA:
            run(s)
        finish(tiles)
        for k in range(8):
            mixB[k] = m2[("mix", k)]
        main_banks[:] = [0, 1, 2, 3]
        for s in outB:
            run(s)
        ffn_mem["start"] = (done["dve"], count["dve"])
        ffn_mem["start2"] = (done["pe"], count["pe"])
        ffn_mem["t_pad"] = [memset(ffn_mem["pad"][:, i, 0:2], 0.0, [ffn_mem["start"], ffn_mem["start2"], (done["act"], count["act"])])
                            for i in range(4)]
        up1[0].hook = norm2.finish
        for s in up1:
            run(s)
        s_mem = semaphore("s_mem")
        t_mem = dma(MEMR[:], A["memT"].rearrange("(k p) t -> p k t", p=P), s_mem, [(done["pool"], ffn_mem["t_pad"][0][1])])
        for k in range(KD):
            norm_m.tile(k, MEMR[:, k, :], t_mem)
        norm_m.finish()
        for s in down1:
            run(s)
        main_banks[:] = [0, 1, 2]
        over_ = [(done["pe"], count["pe"]), (done["act"], count["act"]), (done["dve"], count["dve"])]
        t_con2[0] = dma(con2[:], A["con"][:, NCON1:NCON], semaphore("s_con2"), over_, engine="act")
        b2["cpad0"] = memset(cpad[:, 0:2], 0.0, over_)
        mem_slabs[0].hook = start2
        for s in mem_slabs:
            run(s)
        in2[0].hook = norm_g.finish
        att_gen = attention()
        background.append(att_gen)
        for s in in2:
            run(s, 2)
        finish(att_gen)
        for i in range(3):
            yc[i] = b2[("yc", i)]
        main_banks[:] = [0, 1, 2, 3, 4, 5]
        for s in out2:
            run(s)
        main_banks[:] = [0, 1, 2, 3]
        for s in wo2:
            run(s)
        over_ = [(done["pe"], count["pe"]), (done["act"], count["act"]), (done["dve"], count["dve"])]
        ffn_mem2["start"] = over_[2]
        ffn_mem2["t_pad"] = [memset(ffn_mem["pad"][:, i, 0:2], 0.0, over_) for i in range(4)]
        up2[0].hook = norm_h.finish
        for s in up2:
            run(s)
        for s in down2:
            run(s)
        norm_o.finish()
        s_out = semaphore("s_out")
        out_k = out.rearrange("(k p) t -> k p t", p=P)
        for k in range(KD):
            t = stt(H2[k], H2[k], vcol("g_final", k), rstd[:, 0:T2], MUL, MUL, [norm_o.rstd, t_vec])
            t = dma(out_k[k], H2[k], s_out, [t])
        queues["sp"].append((None, [t], None, 0))
        block = ctx.enter_context(nc.Block())

        def emit(engine, name):
            seen = {}
            for issue, waits, sem, inc in queues[name]:
                need = {}
                for s, v in waits:
                    if seen.get(id(s), 0) < v:
                        need[id(s)] = (s, max(v, need.get(id(s), (s, 0))[1]))
                for i, (s, v) in need.items():
                    engine.wait_ge(s, v)
                    seen[i] = v
                if issue is None:
                    continue
                ins = issue(engine)
                if sem is not None:
                    ins.then_inc(sem, inc)

        @block.sync
        def _(e):
            emit(e, "sp")

        @block.tensor
        def _(e):
            emit(e, "pe")

        @block.scalar
        def _(e):
            emit(e, "act")

        @block.vector
        def _(e):
            emit(e, "dve")

        @block.gpsimd
        def _(e):
            emit(e, "pool")


def kernel(**inputs):
    import concourse.bacc as bacc
    from concourse import mybir
    from concourse.bass_utils import run_bass_kernel_spmd

    a = {n: np.asarray(v) for n, v in inputs.items()}

    def rows(x):
        return np.reshape(x, (-1, P)).T

    laid = {
        "hT": np.concatenate([a["meta_tokens"], a["x"][0]], axis=0).T,
        "memT": a["mem_2"][0].T,
        "vec": np.concatenate([
            rows(a["norm1_w"]), rows(a["hg_norm_w"]), rows(a["m2_conv_w"]), rows(a["m2_conv_b"]), rows(a["m2_norm_w"]),
            rows(np.repeat(a["m2_d"][0], 64)), rows(a["norm2_w"]), rows(a["final_norm_w"]), rows(a["ffn_conv_w"]),
            rows(a["ffn_conv_b"]), rows(a["hg_lb_logits"]), rows(a["b_gate_2"]), rows(a["conv_w_short_2"]),
            rows(a["g_mix_2"]), rows(a["g_mem_2"]), rows(a["g_ffn_2"]), rows(a["conv_w_ffn_2"]), rows(a["g_final_2"]),
        ], axis=1),
        "heads": np.stack([a["m2_dt_bias"][0], a["m2_a_log"][0]], axis=1),
    }
    laid["con"], laid["chunk_mask"] = constants()
    for n in ("w_in", "w_out", "ffn_w_up", "ffn_w_down", "w_in_2", "w_att_out_2", "w_conv_out_2", "w_mem_out_2",
              "w_o_2", "w_mem_kv_2", "w_up_2", "w_down_2"):
        laid[n] = a[n][0]
    nc = bacc.Bacc("TRN2", target_bir_lowering=False, num_devices=1)
    arrays, aps = {}, {}
    for n, v in laid.items():
        v = np.ascontiguousarray(v)
        arrays[f"in_{n}"] = v
        aps[n] = nc.dram_tensor(f"in_{n}", v.shape, mybir.dt.from_np(v.dtype), kind="ExternalInput").ap()
    out = nc.dram_tensor("out_T", (D, T2), mybir.dt.float32, kind="ExternalOutput").ap()
    build_program(nc, aps, out)
    r = run_bass_kernel_spmd(nc, [arrays], core_ids=[0])
    return np.ascontiguousarray(r.results[0]["out_T"].T)[None]
```

```python
from contextlib import ExitStack

import numpy as np

P = 128
D = 1024
KD = D // P
META, SEQ = 16, 256
T1 = META + SEQ
T2 = SEQ
SKIP = META - 2
T1F = T1 - SKIP
FF = 2816
MF = FF // P
HEADS = 8
CHUNK = 16
NCH = T1 // CHUNK
WIN = 2 * CHUNK
M2H = 16
GN = 128
EPS = 1e-6
TOPK = 64
ATT_HEADS, IDX_HEADS, CROSS_HEADS = 6, 8, 4
ROT_A, ROT_I = 8, 4
THETA = 500000.0
FILL = -3.0e38
TAKEN = -3.4e38
PENALTY = -1.0e30

C_Q, C_F, C_I, C_G, C_Z, C_X, C_B, C_C, C_DT = 0, 1024, 2048, 3072, 4096, 5120, 6144, 6400, 6656
C2_Q, C2_K, C2_V, C2_QI, C2_KI, C2_WI, C2_BG, C2_CG, C2_U, C2_QC, C2_GATE = (
    0, 384, 512, 640, 896, 928, 936, 1320, 1704, 2088, 2344)

VEC_PARTS = [("norm1", 8), ("hg_norm", 8), ("m2_conv", 48), ("m2_conv_b", 12), ("m2_norm", 8), ("m2_d", 8),
             ("norm2", 8), ("final1", 8), ("f1_conv", 132), ("f1_conv_b", 44), ("lb", 16), ("b_gate", 24),
             ("short", 9), ("g_mix", 8), ("g_mem", 8), ("g_ffn", 8), ("f2_conv", 132), ("g_final", 8)]
VEC, NVEC = {}, 0
for _n, _w in VEC_PARTS:
    VEC[_n] = NVEC
    NVEC += _w

CON_PARTS = [("ident", P), ("ones", T1), ("reset", 2 * T1), ("eps", 1),
             ("rot_a", P), ("rot_i", P), ("cos_a", T2), ("sin_a", T2), ("cos_i", T2), ("sin_i", T2)]
CON, NCON = {}, 0
for _n, _w in CON_PARTS:
    CON[_n] = NCON
    NCON += _w
NCON1 = CON["rot_a"]


def constants():
    c = np.zeros((P, NCON), np.float32)
    c[:, CON["ident"]:CON["ident"] + P] = np.eye(P)
    c[:, CON["ones"]:CON["ones"] + T1] = 1.0
    for rot, cos, sin, half, dim in (("rot_a", "cos_a", "sin_a", ROT_A, 64), ("rot_i", "cos_i", "sin_i", ROT_I, 32)):
        freq = np.float32(THETA) ** (-np.arange(half, dtype=np.float32) / np.float32(half))
        ang = np.arange(T2, dtype=np.float32)[:, None] * freq.astype(np.float32)[None, :]
        c[:, CON[cos]:CON[cos] + T2] = 1.0
        for base in range(0, P, dim):
            for j in range(half):
                a, b = base + j, base + half + j
                for p in (a, b):
                    c[p, CON[cos]:CON[cos] + T2] = np.cos(ang[:, j])
                    c[p, CON[sin]:CON[sin] + T2] = np.sin(ang[:, j])
                c[b, CON[rot] + a] = -1.0
                c[a, CON[rot] + b] = 1.0
    reset = np.ones(2 * T1, np.float32)
    reset[::CHUNK] = 0.0
    c[:, CON["reset"]:CON["reset"] + 2 * T1] = reset
    c[:, CON["eps"]] = EPS
    m = np.zeros((P, T1), np.int32)
    for col in range(T1):
        win, j, r = col // 64, col % 64 // CHUNK, col % CHUNK
        m[32 * j:32 * j + r + 1, col] = 1
    return c, m


def build_program(nc, A, out):
    import concourse.bass as bass
    from concourse import mybir

    F, R, I32 = mybir.dt.float32, mybir.dt.float32r, mybir.dt.int32
    ALU, ACT, AX = mybir.AluOpType, mybir.ActivationFunctionType, mybir.AxisListType
    MUL, ADD, SUB, MAX, MIN = ALU.mult, ALU.add, ALU.subtract, ALU.max, ALU.min
    ctx = ExitStack()
    with ctx:
        queues = {n: [] for n in ("sp", "pe", "act", "dve", "pool")}
        done = {n: ctx.enter_context(nc.semaphore(f"{n}_done")) for n in ("pe", "act", "dve", "pool")}
        count = dict.fromkeys(done, 0)

        def put(engine, issue, after=(), signal=True):
            waits = [t for t in after if t is not None]
            if signal:
                count[engine] += 1
                queues[engine].append((issue, waits, done[engine], 1))
                return done[engine], count[engine]
            queues[engine].append((issue, waits, None, 0))
            return None

        dma_count = {}

        def dma(dst, src, sem, after=(), engine="sp"):
            queues[engine].append((lambda e: e.dma_start(dst, src), [t for t in after if t is not None], sem, 16))
            dma_count[id(sem)] = dma_count.get(id(sem), 0) + 16
            return sem, dma_count[id(sem)]

        def semaphore(name):
            return ctx.enter_context(nc.semaphore(name))

        def mm(o, lhsT, rhs, start, stop, after=(), signal=False):
            return put("pe", lambda e: e.matmul(o, lhsT, rhs, start=start, stop=stop, skip_group_check=True),
                       after, signal)

        def transpose(o, i, ident, after=(), signal=False):
            return put("pe", lambda e: e.transpose(o, i, ident), after, signal)

        def act(o, i, func, after=(), scale=1.0, bias=0.0, accum=None):
            if accum is None:
                return put("act", lambda e: e.activation(o, i, func, bias=bias, scale=scale), after)
            return put("act", lambda e: e.activation(o, i, func, bias=bias, scale=scale, accum_out=accum), after)

        def tt(o, a, b, op, after=(), engine="dve"):
            return put(engine, lambda e: e.tensor_tensor(o, a, b, op), after)

        def ts(o, a, s1, op0, s2=None, op1=None, after=(), engine="dve"):
            if op1 is None:
                return put(engine, lambda e: e.tensor_scalar(o, a, s1, None, op0), after)
            return put(engine, lambda e: e.tensor_scalar(o, a, s1, s2, op0, op1), after)

        def stt(o, a, s, b, op0, op1, after=()):
            return put("dve", lambda e: e.scalar_tensor_tensor(out=o, in0=a, scalar=s, in1=b, op0=op0, op1=op1), after)

        def copy(o, i, after=(), engine="dve"):
            return put(engine, lambda e: e.tensor_copy(o, i), after)

        def memset(o, v, after=(), engine="pool"):
            return put(engine, lambda e: e.memset(o, v), after)

        top = [(nc.sbuf_base + 63) // 64 * 64]
        LIMIT = nc.sbuf_top - 64

        def size(shape):
            return int(np.prod(shape[1:])) * 4

        def place(name, shape, dt, cursor):
            t = nc.alloc_sbuf_tensor_at(name, list(shape), dt, offset=cursor[0])
            cursor[0] += (size(shape) + 63) // 64 * 64
            assert cursor[0] <= LIMIT, (name, cursor[0], LIMIT)
            return t

        def keep(name, shape, dt=F):
            return place(name, shape, dt, top)

        NRAW, NSPLIT, SLAB = 4, 3, 2048
        raw = [keep(f"w_raw{i}", [P, SLAB]) for i in range(NRAW)]
        w_high = [keep(f"w_high{i}", [P, SLAB], R) for i in range(NSPLIT)]
        w_low = [keep(f"w_low{i}", [P, SLAB], R) for i in range(NSPLIT)]
        con = keep("con", [P, NCON1])
        vec = keep("vec", [P, NVEC])
        chunk_mask = keep("chunk_mask", [P, T1], I32)
        heads16 = keep("heads16", [M2H, 8])
        H = keep("H", [P, KD, T1])
        XH = keep("XH", [P, KD, T1], R)
        XL = keep("XL", [P, KD, T1], R)
        NSQ = 3
        SQ = keep("SQ", [P, NSQ, T1])
        ACC = keep("ACC", [P, T1])
        rstd = keep("rstd", [P, T1])
        lnv = keep("lnv", [P, T1])

        def con_(name, w, rows=P):
            return con[0:rows, CON[name]:CON[name] + w]

        def vcol(name, i):
            return vec[:, VEC[name] + i:VEC[name] + i + 1]

        ident, ones, eps = con_("ident", P), con_("ones", T1), con_("eps", 1)
        banks = [ctx.enter_context(nc.psum_tensor(f"bank{i}", [P, 512], F)) for i in range(8)]
        bank_free = [None] * 8

        s_first = [semaphore(f"s_first{i}") for i in range(6)]
        t_vec = dma(vec[:], A["vec"], s_first[0])
        t_h = []
        for k in range(0, KD, 4):
            t = dma(H[:, k:k + 4, :], A["hT"].rearrange("(k p) t -> p k t", p=P)[:, k:k + 4, :], s_first[1 + k // 4])
            t_h += [t] * 4
        t_con = dma(con[:], A["con"][:, 0:NCON1], s_first[3], [t_h[0]], engine="act")
        t_mask = dma(chunk_mask[:], A["chunk_mask"], s_first[4], engine="act")
        t_hd = dma(heads16[:, 0:2], A["heads"], s_first[5], engine="act")

        background = []
        held_back = []

        def later(issue, ticks=3):
            cell = [None]

            def go():
                cell[0] = issue()
            held_back.append([ticks, go])
            return cell

        def flush():
            while held_back:
                held_back.pop(0)[1]()

        def advance():
            for g in list(background):
                if next(g, "end") == "end":
                    background.remove(g)

        def tick(steps):
            for h in list(held_back):
                h[0] -= 1
                if h[0] <= 0:
                    held_back.remove(h)
                    h[1]()
            for _ in range(steps):
                advance()

        def finish(*gens):
            for g in gens:
                while g in background:
                    tick(1)

        slabs = []

        class Slab:

            def __init__(self, nk, width, pieces, x, tokens, parts, first=True, last=True, hook=None):
                assert nk * width <= SLAB
                self.nk, self.width, self.pieces = nk, width, pieces
                self.x, self.tokens, self.parts, self.first, self.last, self.hook = x, tokens, parts, first, last, hook
                self.early = None
                self.n = len(slabs)
                slabs.append(self)

        s_raw = [semaphore(f"s_raw{i}") for i in range(NRAW)]
        raw_free = [()] * NRAW
        split_free = [None] * NSPLIT
        landed, halves = {}, {}

        def view(t, s):
            return t[:, 0:s.nk * s.width].rearrange("p (k n) -> p k n", k=s.nk)

        def load(n):
            s = slabs[n]
            for i, (c0, w, src, *rows) in enumerate(s.pieces):
                dst = view(raw[n % NRAW], s)[slice(*rows) if rows else slice(0, P), :, c0:c0 + w]
                landed[n] = dma(dst, src, s_raw[n % NRAW], raw_free[n % NRAW] if i == 0 else ())



        def split(n, half):
            s = slabs[n]
            m, middle, q = n % NSPLIT, (s.nk + 1) // 2 * s.width, s.nk * s.width
            c = slice(0, middle) if half == 0 else slice(middle, q)
            r = raw[n % NRAW]
            th = act(w_high[m][:, c], r[:, c], ACT.Copy, [landed[n], split_free[m]])
            tl = tt(w_low[m][:, c], r[:, c], w_high[m][:, c].bitcast(F), SUB, [th, split_free[m]], "dve" if n <= 1 else "pool")
            raw_free[n % NRAW] = (th, tl) if half == 0 else (*raw_free[n % NRAW], th, tl)
            halves[n, half] = (th, tl)

        main_banks = [0, 1, 2]
        turn = [0]
        open_banks = {}
        primed = [0, 0]
        ran = [0]

        def prime(upto_split, whole=False):
            while primed[1] < min(2 * upto_split, 2 * len(slabs)):
                n, half = primed[1] // 2, primed[1] % 2
                while primed[0] < min(n + NRAW, len(slabs)):
                    load(primed[0])
                    primed[0] += 1
                if half == 1 and n == upto_split - 1 and not whole:
                    return
                split(n, half)
                primed[1] += 1

        def run(s, steps=1, every=2):
            assert s.n == ran[0], "slabs run in the order in which they are made"
            ran[0] += 1
            prime(s.n + NSPLIT)
            m = s.n % NSPLIT
            hi, lo = view(w_high[m], s), view(w_low[m], s)
            xh, xl, k0, t0, x_tokens = s.x
            tok = None
            middle = (s.nk + 1) // 2
            for key, c0, M, read in s.parts:
                if s.first:
                    b = main_banks[turn[0] % len(main_banks)]
                    turn[0] += 1
                    open_banks[key] = b
                b = open_banks[key]
                o = banks[b][0:M, 0:s.tokens]
                for k in range(s.nk):
                    th, tl = halves[s.n, int(k >= middle)]
                    x1, x2 = xh[:, k0 + k, t0:t0 + s.tokens], xl[:, k0 + k, t0:t0 + s.tokens]
                    begin, end = s.first and k == 0, s.last and k == s.nk - 1
                    last_of_slab = k == s.nk - 1
                    mm(o, hi[:, k, c0:c0 + M], x1, begin, False, [th, x_tokens[k0 + k][0], bank_free[b] if begin else None])
                    mm(o, hi[:, k, c0:c0 + M], x2, False, False, [x_tokens[k0 + k][1]])
                    tok = mm(o, lo[:, k, c0:c0 + M], x1, False, end, [tl], signal=last_of_slab)
                    if k == middle - 1:
                        prime(s.n + NSPLIT, whole=True)
                    if k % every == every - 1 and k != s.nk - 1:
                        tick(steps)
                        if s.early is not None and k >= 3:
                            s.early()
                            s.early = None
                if s.hook is not None:
                    s.hook()
                    s.hook = None
                if s.last:
                    bank_free[b] = read(banks[b], tok)
                tick(steps)
            split_free[m] = tok

        def columns(w, c, n, k0=0, nk=KD):
            return w[k0 * P:(k0 + nk) * P, c:c + n].rearrange("(k p) n -> p k n", p=P)

        sq_cell = [None] * NSQ

        class Acc:

            def __init__(self, t):
                self.sum, self.cell, self.token = t, None, None

        shared_acc = Acc(ACC)
        STAT = 7

        def rsqrt_mean(o, total, n, after):
            a = act(lnv[:, 0:o.shape[-1]], total, ACT.Ln, after, scale=1.0 / n, bias=eps)
            return act(o, lnv[:, 0:o.shape[-1]], ACT.Exp, [a], scale=-0.5), a

        def square_sum(h, k, first, last, T, after, bank=STAT, engine="act", adder="dve", ticks=3, acc=None):
            acc = acc or shared_acc
            i = k % NSQ
            o = acc.sum[:, 0:T] if first and not last else SQ[:, i, 0:T]
            if (sq_cell[i] and sq_cell[i][0] is None) or (acc.cell and acc.cell[0] is None and first):
                flush()
            free = (acc.cell and acc.cell[0]) if first and not last else (sq_cell[i] and sq_cell[i][0])
            if engine == "act":
                a = act(o, h, ACT.Square, [after, free])
            else:
                a = tt(o, h, h, MUL, [after, free], engine)
            if first and not last:
                acc.token = a
                return None
            if not last:
                acc.token = tt(acc.sum[:, 0:T], acc.sum[:, 0:T], SQ[:, i, 0:T], ADD, [a, acc.token], adder)
                sq_cell[i] = [acc.token]
                return None
            summed = acc.token

            def on_pe():
                if not first:
                    mm(banks[bank][:, 0:T], ones[:, 0:P], acc.sum[:, 0:T], True, False, [summed, t_con, bank_free[bank]])
                return mm(banks[bank][:, 0:T], ones[:, 0:P], SQ[:, i, 0:T], first, True,
                          [a, t_con, bank_free[bank] if first else None], signal=True)
            sq_cell[i] = later(on_pe, ticks)
            if not first:
                acc.cell = sq_cell[i]
            return sq_cell[i]

        def scaled_parts(k, h, gain, T, after, free=None, hi=None, lo=None):
            hi, lo = hi or XH, lo or XL
            a = act(hi[:, k, 0:T], h, ACT.Copy, [after, free], scale=gain)
            b = stt(lo[:, k, 0:T], h, gain, hi[:, k, 0:T].bitcast(F), MUL, SUB, [a])
            return a, b

        def parts_of(k, v, hi, lo, after, T, scale=None):
            if scale is None:
                a = act(hi[:, k, 0:T], v, ACT.Copy, [after])
                b = tt(lo[:, k, 0:T], v, hi[:, k, 0:T].bitcast(F), SUB, [a])
            else:
                a = act(hi[:, k, 0:T], v, ACT.Copy, [after], scale=scale)
                b = stt(lo[:, k, 0:T], v, scale, hi[:, k, 0:T].bitcast(F), MUL, SUB, [a])
            return a, b

        class Normed:

            def __init__(self, T, gain, hi=None, lo=None, factor=None, bank=None, acc=None):
                self.acc = acc
                self.T, self.gain, self.hi, self.lo, self.bank = T, gain, hi, lo, STAT if bank is None else bank
                self.factor = factor if factor is not None else rstd
                self.tokens, self.sum, self.rstd = [None] * KD, None, None

            def tile(self, k, h, after, engine="act", adder="dve", ticks=3):
                self.tokens[k] = scaled_parts(k, h, vcol(self.gain, k), self.T, after, None, self.hi, self.lo)
                self.sum = square_sum(h, k, k == 0, k == KD - 1, self.T, after, self.bank, engine, adder, ticks, self.acc)

            def finish(self):
                if self.sum[0] is None:
                    flush()
                t = self.sum[0]
                self.rstd, bank_free[self.bank] = rsqrt_mean(self.factor[:, 0:self.T], banks[self.bank][:, 0:self.T], D,
                                                            [t, last_rstd_use[0]])

        last_rstd_use = [None]

        small = keep("small", [P, 64])
        lb, omlb = small[:, 0:8], small[:, 8:16]
        l0, l1 = vec[:, VEC["lb"]:VEC["lb"] + 8], vec[:, VEC["lb"] + 8:VEC["lb"] + 16]
        t = tt(small[:, 16:24], l0, l1, MAX, [t_vec])
        t1 = tt(small[:, 24:32], l0, small[:, 16:24], SUB, [t])
        t2 = tt(small[:, 32:40], l1, small[:, 16:24], SUB, [t])
        t3 = act(small[:, 24:40], small[:, 24:40], ACT.Exp, [t1, t2])
        t = tt(small[:, 40:48], small[:, 24:32], small[:, 32:40], ADD, [t3])
        t = put("dve", lambda e: e.reciprocal(small[:, 48:56], small[:, 40:48]), [t])
        t = tt(lb, small[:, 24:32], small[:, 48:56], MUL, [t])
        t_lb = ts(omlb, lb, -1.0, MUL, 1.0, ADD, [t])
        nconv = 48 + 12
        conv_half = keep("conv_half", [P, nconv])
        t_half = ts(conv_half[:], vec[:, VEC["m2_conv"]:VEC["m2_conv"] + nconv], 0.5, MUL, after=[t_vec])
        bgate = vec[:, VEC["b_gate"]:VEC["b_gate"] + 24]
        t_bgate = ts(bgate, bgate, 0.5, MUL, after=[t_vec])

        norm1 = Normed(T1, "norm1")
        xin = (XH, XL, 0, 0, norm1.tokens)

        def dt_reader(bank, tok):
            t = tt(DT[0][:], bank[0:M2H, 0:T1], rstd[0:M2H, :], MUL, [tok, norm1.rstd])
            last_rstd_use[0] = t
            m2["dt_raw"] = t
            return t
        m2 = {}
        dt_slab = Slab(KD, M2H, [(0, M2H, columns(A["w_in"], C_DT, M2H))], xin, T1, [("dt", 0, M2H, dt_reader)],
                       hook=norm1.finish)
        prime(1)
        for k in range(KD):
            norm1.tile(k, H[:, k, :], t_h[k], "pool")

        phase = top[0]
        cur = [phase]
        O_all = place("O_all", [P, HEADS, T1], F, cur)
        G_all = place("G_all", [P, HEADS, T1], F, cur)
        after_og = cur[0]
        W2 = 2 * T1
        f_, k_, e1, q_ = (place(n, [P, W2], F, cur) for n in ("hg_f", "hg_k", "hg_e", "hg_q"))
        bc = f_
        WP = NCH * WIN
        kinv, kend, v_ = (place(n, [P, 2 * WP], F, cur) for n in ("hg_kinv", "hg_kend", "hg_v"))
        qth = place("hg_tanh", [P, W2], F, cur)
        kx = place("hg_kx", [P, W2], F, cur)
        qdec = [place(f"hg_qdec{i}", [P, W2], F, cur) for i in range(2)]
        decay = [place(f"hg_decay{i}", [P, 2 * NCH], F, cur) for i in range(2)]
        ktok = [place(f"hg_ktok{i}", [P, 4 * P], F, cur) for i in range(2)]
        vtok = [place(f"hg_vtok{i}", [P, 5 * P], F, cur) for i in range(2)]
        score = [place(f"hg_score{i}", [P, T1], F, cur) for i in range(2)]
        state = place("hg_state", [P, NCH // 2, P], F, cur)
        hg_end = cur[0]
        t_pads0 = [memset(t[:], 0.0) for t in (kinv, kend, v_)]
        t_score0 = [memset(score[i][:], 0.0) for i in range(2)]
        cur = [after_og]
        MAH = place("MAH", [P, 8, T1], R, cur)
        MAL = place("MAL", [P, 8, T1], R, cur)
        MBH = place("MBH", [P, 8, T1], R, cur)
        MBL = place("MBL", [P, 8, T1], R, cur)
        Z_ = place("m2_Z", [P, 4, T1], F, cur)
        cur = [max(cur[0], hg_end)]
        zth = place("m2_zth", [P, T1], F, cur)
        PADW = T1 + 3
        npad = 2
        mpad = place("m2_pad", [P, npad, PADW], F, cur)
        mcv = place("m2_cv", [P, 2, T1], F, cur)
        mth = place("m2_th", [P, 2, T1], F, cur)
        BC = place("m2_BC", [P, 4, T1], F, cur)
        CBW = T1 + 144 + 16
        CBT = place("m2_CBT", [P, 2, CBW], F, cur)
        dtT = place("m2_dtT", [P, 3 * M2H], F, cur)
        nacT = place("m2_nacT", [P, 3 * M2H], F, cur)
        DT = [place(f"m2_dt{i}", [M2H, T1], F, cur) for i in range(4)]
        over = [phase]
        SEG = [place(f"m2_SEG{i}", [P, CBW], F, c) for i, c in enumerate((over, cur))]
        MT = [place(f"m2_MT{i}", [P, CBW], F, c) for i, c in enumerate((over, cur))]
        XTOK = place("m2_XTOK", [P, 3 * P], F, over)
        X_ = place("m2_X", [P, 4, T1], F, over)
        Y_ = place("m2_Y", [P, 4, T1], F, over)
        rg = place("m2_rg", [P, T1], F, over)
        assert over[0] <= after_og
        t_pad = [memset(mpad[:, i, 0:3], 0.0) for i in range(npad)]

        hg = {}

        def pair_slab(col, p, dests, scale=None, name=None, hook=None, free=None):
            def reader(j):
                def read(bank, tok):
                    o = dests[j]
                    extra = free() if free else ()
                    if name == "v":
                        t = tt(o, chunks(bank[:, 0:T1]), chunks(rstd[:]), MUL, [tok, norm1.rstd, t_pads0[2], *extra])
                    elif scale is None:
                        t = tt(o, bank[:, 0:T1], rstd[:], MUL, [tok, norm1.rstd, *extra])
                    else:
                        t = stt(o, bank[:, 0:T1], scale, rstd[:], MUL, MUL, [tok, norm1.rstd, *extra])
                    hg[(name, p, j)] = t
                    last_rstd_use[0] = t
                    return t
                return read
            return Slab(KD, 256, [(0, 256, columns(A["w_in"], col + 256 * p, 256))], xin, T1,
                        [((name, p, 0), 0, P, reader(0)), ((name, p, 1), P, P, reader(1))], hook=hook)

        def halves_of(t):
            return [t[:, 0:T1], t[:, T1:W2]]

        def chunks(t):
            return t.rearrange("p (c s) -> p c s", s=CHUNK)

        def padded(t):
            return t.rearrange("p (c s) -> p c s", s=WIN)[:, :, 0:CHUNK]

        def hg_gates(p):
            prev = hg.get(("prep_done", p - 1))
            tf = [hg[("f", p, j)] for j in range(2)]
            a = act(e1[:], f_[:], ACT.Exp, [*tf, prev], scale=-1.0)
            yield
            b = ts(e1[:], e1[:], 1.0, ADD, after=[a])
            b = put("dve", lambda e: e.reciprocal(k_[:], e1[:]), [b, prev])
            yield
            ln = []
            for j in range(2):
                h = 2 * p + j
                ln.append(ts(f_[:, j * T1:(j + 1) * T1], k_[:, j * T1:(j + 1) * T1], omlb[:, h:h + 1], MUL,
                             lb[:, h:h + 1], ADD, after=[b, t_lb, a]))
            c = ts(k_[:], f_[:], -1.0, MUL, 1.0, ADD, after=ln)
            d = act(f_[:], f_[:], ACT.Ln, [*ln, c])
            yield
            s = put("dve", lambda e: e.tensor_tensor_scan(bc[:], con_("reset", W2), f_[:], 0.0, MUL, ADD),
                    [d, t_con])
            yield
            g = act(e1[:], bc[:], ACT.Exp, [s])
            hg[("eb", p)] = g
            yield
            while ("qa", p) not in hg:
                yield
            th, qt = hg[("qa", p)]
            q = tt(qdec[p % 2][:], q_[:], e1[:], MUL, [g, qt, hg.get(("qdec_free", p - 2))])
            dd = copy(decay[p % 2][:].rearrange("p (c o) -> p c o", o=1), chunks(e1[:])[:, :, CHUNK - 1:CHUNK],
                      [g, hg.get(("qdec_free", p - 2))])
            hg[("q_free", p)] = q
            hg[("qdec", p)] = q
            hg[("decay", p)] = dd
            yield
            i = act(e1[:], bc[:], ACT.Exp, [q, dd], scale=-1.0)
            last = chunks(bc[:])[:, :, CHUNK - 1:CHUNK].to_broadcast([P, 2 * NCH, CHUNK])
            w = tt(chunks(kx[:]), last, chunks(bc[:]), SUB, [s, hg.get(("prep_done", p - 1))])
            hg[("f_free", p)] = (w, i)
            w = act(kx[:], kx[:], ACT.Exp, [w])
            yield
            ki = tt(padded(kinv[:]), chunks(k_[:]), chunks(e1[:]), MUL, [i, c, hg.get(("kinv_free", p - 1)), t_pads0[0]])
            ke = tt(padded(kend[:]), chunks(k_[:]), chunks(kx[:]), MUL, [w, c, hg.get(("kend_free", p - 1)), t_pads0[1]])
            hg[("kinv", p)], hg[("kend", p)] = ki, ke
            hg[("prep_done", p)] = ke
            yield

        def silu_from_half(o, half, scratch, after, extra=()):
            a = act(scratch, half, ACT.Tanh, after)
            return stt(o, scratch, 1.0, half, ADD, MUL, [a, *extra])

        def hg_head(p, j):
            h = 2 * p + j
            O = STAT
            head_prev = hg.get(("head_done", p - 1, j))
            base_k, base_v = kend[:, j * WP:(j + 1) * WP], v_[:, j * WP:(j + 1) * WP]
            queries = qdec[p % 2][:, j * T1:(j + 1) * T1]
            ndecay = decay[p % 2][:, j * NCH:j * NCH + NCH - 1].rearrange("p (r two) -> p r two", two=2)
            pair_decay = small[:, 16 + 8 * j:24 + 8 * j]

            def windows(src, dst, after, free, bank):
                for T in range(4):
                    tk = transpose(banks[bank][:, T * P:(T + 1) * P], src[:, T * P:(T + 1) * P], ident,
                                   [*after, t_con, bank_free[bank]] if T == 0 else (), signal=T == 3)
                c = act(dst, banks[bank][:, :], ACT.Copy, [tk, free])
                bank_free[bank] = c
                return tk, c
            while ("kend", p) not in hg:
                yield
            for _ in range(3 if j == 0 else 0):
                yield
            for T in range(5):
                ncol = 64 if T < 4 else CHUNK
                rows = P if T < 4 else CHUNK
                mm(banks[6][0:rows, 64 * T:64 * T + ncol], kinv[:, j * WP + T * P:j * WP + T * P + rows],
                   queries[:, 64 * T:64 * T + ncol], T == 0, True,
                   [bank_free[6], hg[("kinv", p)], hg[("qdec", p)]] if T == 0 else ())
            for T in range(4):
                mm(banks[5][:, P + 64 * T:P + 64 * T + 64], base_k[:, T * P:(T + 1) * P],
                   queries[:, 64 * T:64 * T + 64], T == 0, True, [bank_free[5], hg[("kend", p)]] if T == 0 else ())
            tk = transpose(banks[5][0:CHUNK, 0:P], base_v[:, 4 * P:4 * P + CHUNK], ident, [hg[("v", p, j)], t_con],
                           signal=True)
            hg[("kinv_free", p)] = tk
            t, cv = windows(base_v, vtok[j][:, 0:4 * P], (), head_prev, 4)
            hg[("v_free", p, j)] = t
            yield
            m1 = put("dve", lambda e: e.copy_predicated(score[j][:, 0:256], chunk_mask[:, 0:256], banks[6][:, 0:256]),
                     [tk, t_mask, t_score0[j], head_prev])
            m2_ = put("dve", lambda e: e.copy_predicated(score[j][0:CHUNK, 256:T1], chunk_mask[0:CHUNK, 256:T1],
                                                         banks[6][0:CHUNK, 256:T1]), [tk])
            bank_free[6] = m2_
            cv2 = act(vtok[j][0:CHUNK, 4 * P:5 * P], banks[5][0:CHUNK, 0:P], ACT.Copy, [tk])
            for row, col in ((0, CHUNK), (64, 48)):
                c_x = act(score[j][row:row + CHUNK, 0:256].rearrange("p (t q) -> p t q", q=64)[:, :, col:col + CHUNK],
                        banks[5][row:row + CHUNK, P:3 * P].rearrange("p (t q) -> p t q", q=64)[:, :, col:col + CHUNK],
                        ACT.Copy, [tk, m1])
            bank_free[5] = c_x
            keys_a = base_k[:, 0:512].rearrange("p (r s) -> p r s", s=2 * WIN)[:, :, 0:CHUNK]
            ks = tt(keys_a, keys_a, ndecay[:, :, 1:2].to_broadcast([P, 8, CHUNK]), MUL, [tk, hg[("decay", p)]])
            queries_b = queries[:, 0:256].rearrange("p (r s) -> p r s", s=WIN)[:, :, CHUNK:WIN]
            qs = tt(queries_b, queries_b, ndecay[:, :, 0:1].to_broadcast([P, 8, CHUNK]), MUL, [tk])
            tt(pair_decay.rearrange("p (r o) -> p r o", o=1), ndecay[:, :, 0:1], ndecay[:, :, 1:2], MUL)
            yield
            yield
            yield
            tk, ck = windows(base_k, ktok[j][:], [ks], head_prev, 3)
            hg[("kend_free", p)] = tk
            yield
            yield
            yield
            for T in range(4):
                for c in range(2):
                    rows = slice(64 * c, 64 * c + 48)
                    tk = mm(banks[3 + c][:, T * P:(T + 1) * P], ktok[j][rows, T * P:(T + 1) * P],
                            vtok[j][rows, T * P:(T + 1) * P], T == 0, True,
                            [bank_free[3 + c], ck, cv] if T == 0 else (), signal=T == 3)
                    hg["u", c] = tk
            yield
            upd = None
            ups = {}
            while hg.get("norm_open"):
                yield
            for T in range(7):
                if T >= 2:
                    S = T - 2
                    ncol = 64 if S < 4 else CHUNK
                    rows = P if S < 4 else CHUNK
                    oc = slice(64 * S, 64 * S + ncol)
                    mm(banks[O][:, oc], vtok[j][0:rows, S * P:(S + 1) * P], score[j][0:rows, oc], S == 0, False,
                       [bank_free[O], m1, m2_, c_x, cv, cv2, qs] if S == 0 else ())
                    for r in range(2 * S, min(2 * S + 2, 9)):
                        if r:
                            end = min((r + 1) * WIN, T1)
                            tk = mm(banks[O][:, r * WIN:end], state[:, r - 1, :], queries[:, r * WIN:end], False, True,
                                    [ups[min(2 * S, 7)]], signal=r == min(2 * S + 1, 8))
                if T < 4:
                    for c in range(2):
                        n = 2 * T + c
                        u = banks[3 + c][:, T * P:(T + 1) * P]
                        if n == 0:
                            upd = copy(state[:, 0, :], u, [hg["u", c], hg.get("state_free")])
                        else:
                            upd = stt(state[:, n, :], state[:, n - 1, :], pair_decay[:, n:n + 1], u, MUL, ADD,
                                      [hg["u", c], upd])
                        ups[n] = upd
                        bank_free[3 + c] = upd
                yield
            hg["state_free"] = tk
            hg[("qdec_free", p)] = tk
            hg[("head_done", p, j)] = tk
            c = act(O_all[:, h, :], banks[O][:, 0:T1], ACT.Copy, [tk])
            total = square_sum(banks[O][:, 0:T1], h, True, True, T1, tk)
            bank_free[O] = (done["act"], count["act"])
            background.append(hg_norm(h, c, total))

        def hg_norm(h, copied, total):
            hg["norm_open"] = True
            rs, i = SQ[:, h % NSQ, :], h % NSQ
            if h % 2 == 0:
                while total[0] is None:
                    yield
                hg["even_sum"] = bank_free[STAT] = act(rs, banks[STAT][:, 0:T1], ACT.Copy, [total[0]])
                hg["norm_open"] = False
                sq_cell[i] = None
                return
            while total[0] is None:
                yield
            before = SQ[:, (h - 1) % NSQ, :]
            a = act(rs, banks[STAT][:, 0:T1], ACT.Ln, [total[0]], scale=1.0 / P, bias=eps)
            bank_free[STAT] = a
            hg["norm_open"] = False
            c = act(before, before, ACT.Ln, [hg["even_sum"]], scale=1.0 / P, bias=eps)
            yield
            roots = [(h - 1, before, act(before, before, ACT.Exp, [c], scale=-0.5)),
                     (h, rs, act(rs, rs, ACT.Exp, [a], scale=-0.5))]
            yield
            for n, r, t in roots:
                while ("ga", n) not in hg:
                    yield
                b = stt(O_all[:, n, :], O_all[:, n, :], vcol("hg_norm", n), r, MUL, MUL, [t, copied, t_vec])
                sq_cell[n % NSQ] = [b]
                hg[("o", n)] = tt(O_all[:, n, :], O_all[:, n, :], G_all[:, n, :], MUL, [b, hg[("ga", n)]])
                yield

        def hg_parts():
            while ("o", HEADS - 1) not in hg:
                yield
            prev = [hg[("head_done", 3, j)] for j in range(2)] + [hg[("o", HEADS - 1)]]
            for h in range(HEADS):
                a = act(MAH[:, h, :], O_all[:, h, :], ACT.Copy, [hg[("o", h)], *prev])
                b = tt(MAL[:, h, :], O_all[:, h, :], MAH[:, h, :].bitcast(F), SUB, [a])
                hg[("mix", h)] = (a, b)
                yield

        hg_slabs = []
        for p in range(4):
            hg_slabs.append((
                pair_slab(C_F, p, halves_of(f_), name="f", free=lambda p=p: hg.get(("f_free", p - 1), ())),
                pair_slab(C_Q, p, halves_of(q_), 0.5, "q", free=lambda p=p: [hg.get(("q_free", p - 1))]),
                pair_slab(C_I, p, [padded(v_[:, j * WP:(j + 1) * WP]) for j in range(2)], name="v",
                          free=lambda p=p: [hg.get(("v_free", p - 1, 0)), hg.get(("v_free", p - 1, 1))]),
                pair_slab(C_G, p, [G_all[:, 2 * p + j, :] for j in range(2)], 0.5, "g")))


        def conv_tile(m, T, K, pad, cv, w, b, after, taps_free=None):
            first = pad[:, K - 1:K - 1 + T]
            if b is None:
                t = act(cv, first, ACT.Copy, [*after, taps_free], scale=w(K - 1))
            else:
                t = act(cv, first, ACT.Identity, [*after, taps_free], scale=w(K - 1), bias=b)
            for k in range(K - 1):
                t = stt(cv, pad[:, k:k + T], w(k), cv, MUL, ADD, [t])
            return t

        pad_turn = [0]
        pad_free, pad_busy = [None] * npad, [False] * npad

        def xbc_reader(m, dest, dest_free):
            def rest(i, t):
                yield
                for k in range(3):
                    t = stt(mcv[:, i, :], mpad[:, i, k:k + T1], conv_half[:, 12 * k + m:12 * k + m + 1], mcv[:, i, :],
                            MUL, ADD, [t])
                yield
                a = act(mth[:, i, :], mcv[:, i, :], ACT.Tanh, [t])
                yield
                m2[("xbc", m)] = pad_free[i] = stt(dest, mth[:, i, :], 1.0, mcv[:, i, :], ADD, MUL, [a, dest_free()])
                pad_busy[i] = False

            def read(bank, tok):
                i = pad_turn[0] % npad
                pad_turn[0] += 1
                while pad_busy[i]:
                    advance()
                pad_busy[i] = True
                t = tt(mpad[:, i, 3:3 + T1], bank[:, 0:T1], rstd[:], MUL, [tok, norm1.rstd, pad_free[i], t_pad[i]])
                last_rstd_use[0] = t
                c = act(mcv[:, i, :], mpad[:, i, 3:3 + T1], ACT.Identity, [t, t_half, pad_free[i]],
                        scale=conv_half[:, 36 + m:37 + m], bias=conv_half[:, 48 + m:49 + m])
                background.append(rest(i, c))
                return t
            return read

        def m2_dt():
            x, e, s, d = DT
            t = ts(x[:], x[:], heads16[:, 0:1], ADD, after=[m2["dt_raw"], t_hd])
            a = act(e[:], x[:], ACT.Abs, [t])
            a = act(e[:], e[:], ACT.Exp, [a], scale=-1.0)
            yield
            b = ts(s[:], e[:], 2.0, ADD, after=[a])
            b = put("dve", lambda e_: e_.reciprocal(s[:], s[:]), [b])
            b = tt(s[:], s[:], e[:], MUL, [b])
            yield
            c = tt(e[:], s[:], s[:], MUL, [b])
            terms = 9
            yield
            c = ts(d[:], e[:], 2.0 / (2 * terms + 1), MUL, after=[c])
            for n in range(terms - 1, 0, -1):
                c = stt(d[:], d[:], 2.0 / (2 * n + 1), e[:], ADD, MUL, [c])
                if n % 2 == 0:
                    yield
            c = stt(d[:], d[:], 2.0, s[:], ADD, MUL, [c])
            c = stt(d[:], x[:], 0.0, d[:], MAX, ADD, [c])
            z = act(heads16[:, 2:3], heads16[:, 1:2], ACT.Exp, [t_hd])
            z = ts(heads16[:, 3:4], heads16[:, 2:3], -1.0, MUL, after=[z])
            z = ts(x[:], d[:], heads16[:, 3:4], MUL, after=[z, c])
            yield
            z = put("dve", lambda e_: e_.tensor_tensor_scan(e[:], con_("ones", T1, M2H), x[:], 0.0, MUL, ADD), [z, t_con])
            m2["acum"] = z
            for _ in range(6):
                yield
            n = None
            for i, (src, tok) in enumerate(((d, c), (e, z))):
                for jt in range(3):
                    rows = P if jt < 2 else 16
                    n = transpose(banks[STAT][0:rows, 48 * i + 16 * jt:48 * i + 16 * jt + 16],
                                  src[:, jt * P:jt * P + rows], con_("ident", M2H, M2H), [tok, bank_free[STAT]],
                                  signal=True)
            yield
            r = None
            for c0, rows in ((0, P), (32, 16)):
                w = 32 if c0 == 0 else 16
                r = ts(dtT[0:rows, c0:c0 + w], banks[STAT][0:rows, c0:c0 + w], 1.0, MUL, after=[n])
                r = ts(nacT[0:rows, c0:c0 + w], banks[STAT][0:rows, 48 + c0:48 + c0 + w], -1.0, MUL, after=[n])
            bank_free[STAT] = r
            m2["rows"] = r

        def m2_scores():
            while ("o", HEADS - 1) not in hg:
                yield
            for g in range(2):
                while ("xbc", 8 + g) not in m2 or ("xbc", 10 + g) not in m2:
                    yield
                yield
                Bt, Ct = BC[:, g, :], BC[:, 2 + g, :]
                for jt, (c0, w, rows) in enumerate(BLOCKS):
                    n = mm(banks[STAT][0:rows, c0:c0 + w], Bt[:, jt * P:jt * P + rows], Ct[:, jt * P:jt * P + w],
                           jt == 0, True, [m2[("xbc", 8 + g)], m2[("xbc", 10 + g)], bank_free[STAT]], signal=jt == 2)
                q1 = copy(CBT[:, g, 0:416], banks[STAT][:, 0:416], [n])
                q2 = copy(CBT[0:16, g, 416:432], banks[STAT][0:16, 416:432], [n])
                bank_free[STAT] = q2
                for jt, (c0, w, rows) in enumerate(BLOCKS):
                    dg = CBT[0:rows, g, c0:c0 + rows]
                    r = put("pool", lambda e_, dg=dg, rows=rows: e_.affine_select(
                        out=dg, in_=dg, compare_op=ALU.is_ge, fill=0.0, base=0, pattern=[[1, rows]],
                        channel_multiplier=-1), [q1, q2])
                m2[("cbt", g)] = r
                yield

        BLOCKS = [(0, T1, P), (T1, T1 - P, P), (2 * T1 - P, T1 - 2 * P, T1 - 2 * P)]

        def m2_heads():
            TR, BB, YB = 3, 4, 5

            def ready(h):
                m = h // 2
                return ("xbc", m) in m2 and ("cbt", m // 4) in m2 and ("z", m) in m2

            head, differences, outputs = 0, None, None
            while head < M2H or differences is not None or outputs is not None:
                new = head if head < M2H and ready(head) else None
                if new is None and differences is None and outputs is None:
                    yield
                    continue
                if new is not None:
                    n = mm(banks[BB][:, 0:T1], con_("ident", M2H, M2H)[:, new:new + 1].to_broadcast([M2H, P]), DT[1][:],
                           True, True, [m2["acum"], bank_free[BB]], signal=True)
                if outputs is not None and outputs % 2 == 0:
                    tr = m2[("xtr", outputs // 2)]
                    c1 = act(XTOK[:, 0:2 * P], banks[TR][:, 0:2 * P], ACT.Copy, [tr, m2.get("xtok_free")])
                    c2 = act(XTOK[0:16, 2 * P:3 * P], banks[TR][0:16, 2 * P:3 * P], ACT.Copy, [tr])
                    bank_free[TR] = m2["xtok"] = c2
                if differences is not None:
                    h, S = differences, SEG[differences % 2]
                    a = act(S[:, 0:416], S[:, 0:416], ACT.Exp, [m2[("seg", h)]])
                    a = act(S[0:16, 416:432], S[0:16, 416:432], ACT.Exp, [m2[("seg", h)]])
                yield
                if new is not None:
                    S, m = SEG[new % 2], new // 2
                    for jt, (c0, w, rows) in enumerate(BLOCKS):
                        s = ts(S[0:rows, c0:c0 + w], banks[BB][0:rows, jt * P:T1],
                               nacT[0:rows, 16 * jt + new:16 * jt + new + 1], ADD, 0.0, MIN,
                               after=[n, m2["rows"], m2.get(("seg_free", new % 2))])
                    bank_free[BB] = m2[("seg", new)] = s
                    if new % 2 == 0:
                        for jt, (c0, w, rows) in enumerate(BLOCKS):
                            m2[("xtr", m)] = transpose(banks[TR][0:rows, jt * P:(jt + 1) * P],
                                                       X_[:, m % 4, jt * P:jt * P + rows], ident,
                                                       [m2[("xbc", m)], bank_free[TR]], signal=True)
                if differences is not None:
                    h, S, M, g = differences, SEG[differences % 2], MT[differences % 2], differences // 8
                    for jt, (c0, w, rows) in enumerate(BLOCKS):
                        s = stt(M[0:rows, c0:c0 + w], S[0:rows, c0:c0 + w], dtT[0:rows, 16 * jt + h:16 * jt + h + 1],
                                CBT[0:rows, g, c0:c0 + w], MUL, MUL,
                                [a, m2["rows"], m2[("cbt", g)], m2.get(("mt_free", h % 2))])
                    m2[("seg_free", h % 2)] = m2[("mt", h)] = s
                yield
                if outputs is not None:
                    h, e, M = outputs, outputs % 2, MT[outputs % 2]
                    for jt, (c0, w, rows) in enumerate(BLOCKS):
                        y = mm(banks[YB][64 * e:64 * e + 64, jt * P:T1], XTOK[0:rows, jt * P + 64 * e:jt * P + 64 * e + 64],
                               M[0:rows, c0:c0 + w], jt == 0, jt == 2, [m2[("mt", h)], m2["xtok"], bank_free[YB]],
                               signal=jt == 2)
                    m2[("mt_free", h % 2)] = m2["xtok_free"] = y
                    if e:
                        background.append(m2_tile(h // 2, y))
                        yield
                yield
                outputs, differences = differences, new
                if new is not None:
                    head += 1

        def m2_tile(m, n):
            g, YB = m // 4, 5
            X, Z, Y = X_[:, m % 4, :], Z_[:, m % 4, :], Y_[:, m % 4, :]
            y = stt(Y, X, vcol("m2_d", m), banks[YB][:, 0:T1], MUL, ADD, [n, t_vec, m2[("xbc", m)], m2.get(("y_free", m - 4))])
            bank_free[YB] = y
            m2[("x_free", m)] = y
            y = tt(Y, Y, Z, MUL, [y, m2[("z", m)]], "pool")
            m2[("z_free", m)] = y
            m2[("tile_done", m)] = True
            yield
            t = square_sum(Y, m, m % 4 == 0, m % 4 == 3, T1, y)
            if m % 4 == 3:
                while t[0] is None:
                    yield
                r, bank_free[STAT] = rsqrt_mean(rg[:], banks[STAT][:, 0:T1], 4 * P, [t[0], m2.get("rg_free")])
                yield
                for i in range(4):
                    k = 4 * g + i
                    b = stt(Y_[:, i, :], Y_[:, i, :], vcol("m2_norm", k), rg[:], MUL, MUL, [r, y])
                    m2[("mix", k)] = parts_of(k, Y_[:, i, :], MBH, MBL, b, T1)
                    m2[("y_free", k)] = m2[("mix", k)][1]
                    yield
                m2["rg_free"] = b
                m2[("group_done", g)] = True

        def z_reader(m):
            def read(bank, tok):
                Z = Z_[:, m % 4, :]
                t = stt(Z, bank[:, 0:T1], 0.5, rstd[:], MUL, MUL, [tok, norm1.rstd, m2.get(("z_free", m - 4))])
                last_rstd_use[0] = t

                def rest():
                    yield
                    a = act(zth[:], Z, ACT.Tanh, [t, m2.get("zth_free")])
                    m2["zth_free"] = m2[("z", m)] = stt(Z, zth[:], 1.0, Z, ADD, MUL, [a])
                background.append(rest())
                return t
            return read
        def slab2(w, col, readers, key, x, T, hook=None, nk=KD, k0=0, first=True, last=True, wk0=0):
            return Slab(nk, P * len(readers), [(0, P * len(readers), columns(w, col, P * len(readers), wk0, nk))],
                        x, T, [((key, i), P * i, P, r) for i, r in enumerate(readers)], first, last, hook)

        none = lambda: None
        b_slab = slab2(A["w_in"], C_B, [xbc_reader(8 + i, BC[:, i, :], none) for i in range(2)], "B", xin, T1)
        c_slab = slab2(A["w_in"], C_C, [xbc_reader(10 + i, BC[:, 2 + i, :], none) for i in range(2)], "C", xin, T1)
        def z_slab(q):
            return slab2(A["w_in"], C_Z + 256 * q, [z_reader(2 * q + i) for i in range(2)], ("z", q), xin, T1)

        def x_slab(q):
            return slab2(A["w_in"], C_X + 256 * q, [xbc_reader(2 * q + i, X_[:, (2 * q + i) % 4, :],
                         lambda m=2 * q + i: m2.get(("x_free", m - 4))) for i in range(2)], ("x", q), xin, T1)

        wo = {}
        norm2 = Normed(T1F, "norm2")

        def add_reader(m, nxt):
            def read(bank, tok):
                t = tt(H[:, m, SKIP:], bank[:, 0:T1F], H[:, m, SKIP:], ADD, [tok, wo.get(m)])
                wo[m] = t
                if nxt is not None:
                    nxt.tile(m, H[:, m, SKIP:], t)
                return t
            return read
        mixA = [None] * 8
        mixB = [None] * 8

        def a_slab(q):
            return slab2(A["w_out"], 256 * q, [add_reader(2 * q + i, None) for i in range(2)], ("oa", q),
                         (MAH, MAL, 0, SKIP, mixA), T1F)
        z_slabs = [z_slab(q) for q in range(2)]
        m2_order = [(kind, q, {"x": x_slab, "z": z_slab, "a": a_slab}[kind](q)) for kind, q in
                    (("x", 0), ("x", 1), ("a", 0), ("z", 2), ("x", 2), ("a", 1), ("z", 3), ("x", 3), ("a", 2), ("a", 3))]
        outB = [slab2(A["w_out"], 256 * q, [add_reader(2 * q + i, norm2) for i in range(2)], ("ob", q),
                      (MBH, MBL, 0, SKIP, mixB), T1F, wk0=8) for q in range(4)]

        def ffn(tag, T, w_up, w_down, conv, conv_b, norm, x, down_reader, mem):
            AH, AL = mem["AH"], mem["AL"]
            acts = [None] * MF
            pad, cv, sg, av = mem["pad"], mem["cv"], mem["sg"], mem["av"]
            NP = 4
            pfree, cfree, afree = [None] * NP, [None] * NP, [None] * 2
            turnp = [0]
            f = {}

            def reader(m, is_val):
                mm_ = m + MF * is_val

                def rest(i, t):
                    yield
                    for k in range(2):
                        t = stt(cv[:, i, 0:T], pad[:, i, k:k + T], vcol(conv, 44 * k + mm_), cv[:, i, 0:T], MUL, ADD, [t])
                    pfree[i] = t
                    yield
                    if not is_val:
                        cfree[i] = f[("gate", m)] = act(sg[:, m % 2, 0:T], cv[:, i, 0:T], ACT.Silu, [t, f.get(("sg", m - 2)), mem["start"]])
                        return
                    j = m % 2
                    s = tt(av[:, j, 0:T], sg[:, j, 0:T], cv[:, i, 0:T], MUL, [t, f[("gate", m)], afree[j], mem["start"]])
                    cfree[i] = f[("sg", m)] = s
                    yield
                    a = act(AH[:, m, 0:T], av[:, j, 0:T], ACT.Copy, [s])
                    yield
                    afree[j] = tt(AL[:, m, 0:T], av[:, j, 0:T], AH[:, m, 0:T].bitcast(F), SUB, [a])
                    acts[m] = (a, afree[j])

                def read(bank, tok):
                    i = turnp[0] % NP
                    turnp[0] += 1
                    t = tt(pad[:, i, 2:2 + T], bank[:, 0:T], rstd[:, 0:T], MUL, [tok, norm.rstd, pfree[i], mem["t_pad"][i]])
                    last_rstd_use[0] = t
                    w, after = vcol(conv, 88 + mm_), [t, cfree[i], mem["start"]]
                    if conv_b:
                        c = act(cv[:, i, 0:T], pad[:, i, 2:2 + T], ACT.Identity, after, scale=w, bias=vcol(conv_b, mm_))
                    else:
                        c = act(cv[:, i, 0:T], pad[:, i, 2:2 + T], ACT.Copy, after, scale=w)
                    background.append(rest(i, c))
                    return t
                return read
            ups, downs = [], []
            for q in range(MF // 2):
                ups.append(slab2(w_up, 256 * q, [reader(2 * q + i, 0) for i in range(2)], (tag, "g", q), x, T))
                ups.append(slab2(w_up, FF + 256 * q, [reader(2 * q + i, 1) for i in range(2)], (tag, "v", q), x, T))
            for q in range(4):
                for k0, nk in ((0, 8), (8, 8), (16, 6)):
                    downs.append(slab2(w_down, 256 * q, [down_reader(2 * q + i) for i in range(2)], (tag, "d", q),
                                       (AH, AL, k0, T - T2, acts), T2, nk=nk, wk0=k0, first=k0 == 0, last=k0 == 16))
            return ups, downs

        cur = [phase]
        ffn_mem = {"AH": place("AH", [P, MF, T1], R, cur), "AL": place("AL", [P, MF, T1], R, cur),
                   "pad": place("ff_pad", [P, 4, T1 + 2], F, cur), "cv": place("ff_cv", [P, 4, T1], F, cur),
                   "sg": place("ff_sg", [P, 2, T1], F, cur), "av": place("ff_av", [P, 2, T1], F, cur)}
        ffn_end = cur[0]

        class Sums:

            def __init__(self, T):
                self.T, self.sum, self.tokens = T, None, [None] * KD

            def tile(self, k, h, after):
                self.tokens[k] = after
                self.sum = square_sum(h, k, k == 0, k == KD - 1, self.T, after)

        Sums.finish = Normed.finish
        norm_f = Sums(T2)
        norm_f.factor, norm_f.bank = rstd, STAT

        def down1_reader(m):
            def read(bank, tok):
                t = tt(H2[m], bank[:, 0:T2], H2[m], ADD, [tok])
                norm_f.tile(m, H2[m], t)
                return t
            return read
        up1, down1 = ffn("f1", T1F, A["ffn_w_up"], A["ffn_w_down"], "f1_conv", "f1_conv_b", norm2,
                         (XH, XL, 0, 0, norm2.tokens), down1_reader, ffn_mem)


        H2 = [H[:, k, META:T1] for k in range(KD)]
        cur = [ffn_end]
        MEMR = place("MEMR", [P, KD, T2], F, cur)
        MEMH = place("MEMH", [P, KD, T2], R, cur)
        MEML = place("MEML", [P, KD, T2], R, cur)
        mem_rstd = place("mem_rstd", [P, T2], F, cur)
        norm_m = Normed(T2, "g_mem", MEMH, MEML, mem_rstd, 6, Acc(place("mem_acc", [P, T2], F, cur)))
        norm_g = Normed(T2, "g_mix", bank=6)
        norm_h = Normed(T2, "g_ffn")
        xin2 = (XH, XL, 0, 0, norm_g.tokens)
        NB = T2 // P

        cur = [phase]
        con2 = place("con2", [P, NCON - NCON1], F, cur)
        con2_ = lambda name, w: con2[:, CON[name] - NCON1:CON[name] - NCON1 + w]
        kmT = place("kmT", [P, 2, T2], F, cur)
        vmtok = place("vmtok", [P, NB, 2 * P], F, cur)
        rraw = place("rraw", [P, 2, T2], F, cur)
        rtmp = place("rtmp", [P, T2], F, cur)
        qiT = place("qiT", [P, 2, T2], F, cur)
        kiT = place("kiT", [P, T2], F, cur)
        qT = place("qT", [P, 3, T2], F, cur)
        kT = place("kT", [P, T2], F, cur)
        vT = place("vT", [P, 2, T2], F, cur)
        vtok2 = place("vtok", [P, NB, P], F, cur)
        wi = place("wi", [IDX_HEADS, T2], F, cur)
        wiT = place("wiT", [P, NB * IDX_HEADS], F, cur)
        relu = place("relu", [P, 4, T2], F, cur)
        sco = place("sco", [P, 2, T2], F, cur)
        pen = place("pen", [P, 2, T2], F, cur)
        max8 = place("max8", [P, 8], F, cur)
        soft = place("soft", [P, 4, 4], F, cur)
        qcT = place("qcT", [P, 2, T2], F, cur)
        prob = relu
        PT = place("PT", [P, 2, 4 * P], F, cur)
        CG = place("CG", [P, 3, T2], F, cur)
        cpad = place("cpad", [P, T2 + 2], F, cur)
        ccv = place("ccv", [P, 3, T2], F, cur)
        ctmp = place("ctmp", [P, T2], F, cur)
        temps_end = cur[0]
        YAH, YAL = place("YAH", [P, 3, T2], R, cur), place("YAL", [P, 3, T2], R, cur)
        YCH, YCL = place("YCH", [P, 3, T2], R, cur), place("YCL", [P, 3, T2], R, cur)
        YMH, YML = place("YMH", [P, 2, T2], R, cur), place("YML", [P, 2, T2], R, cur)
        G2 = place("G2", [P, 24, T2], F, cur)
        cur = [phase]
        MG = place("MG", [P, KD, T2], F, cur)
        MGH, MGL = place("MGH", [P, KD, T2], R, cur), place("MGL", [P, KD, T2], R, cur)
        mtmp = place("mtmp", [P, 2, T2], F, cur)
        assert cur[0] <= temps_end
        b2 = {}

        def scaled(o, bank, tok, norm=None, extra=()):
            norm = norm or norm_g
            t = tt(o, bank[0:o.shape[0], 0:T2], norm.factor[0:o.shape[0], 0:T2], MUL, [tok, norm.rstd, *extra])
            if norm is norm_g:
                last_rstd_use[0] = t
            return t

        def plain(name, o, norm=None):
            def read(bank, tok):
                b2[name] = scaled(o, bank, tok, norm)
                return b2[name]
            return read

        rope_turn = [0]
        rope_cell = [None] * 2

        def roped(name, o, rot, cos, sin):
            def read(bank, tok):
                i = rope_turn[0] % 2
                rope_turn[0] += 1
                if rope_cell[i] is not None and rope_cell[i][0] is None:
                    flush()
                t = scaled(rraw[:, i, :], bank, tok, extra=[rope_cell[i] and rope_cell[i][0]])

                def rotate():
                    n = mm(banks[STAT][:, 0:T2], con2_(rot, P), rraw[:, i, :], True, True,
                           [t, t_con2[0], bank_free[STAT]], signal=True)
                    a = tt(o, rraw[:, i, :], con2_(cos, T2), MUL, [t, t_con2[0]])
                    b = tt(rtmp[:], banks[STAT][:, 0:T2], con2_(sin, T2), MUL, [n])
                    bank_free[STAT] = b
                    b2[name] = tt(o, o, rtmp[:], ADD, [a, b])
                    return b
                rope_cell[i] = later(rotate)
                return t
            return read

        t_con2 = [None]

        def wi_reader(bank, tok):
            t = scaled(wi[:], bank, tok)

            def turn_wi():
                for n in range(NB):
                    r = transpose(banks[STAT][:, n * IDX_HEADS:(n + 1) * IDX_HEADS], wi[:, n * P:(n + 1) * P],
                                  con_("ident", IDX_HEADS, IDX_HEADS), [t, bank_free[STAT]], signal=True)
                b2["wi"] = ts(wiT[:], banks[STAT][:, 0:NB * IDX_HEADS], (IDX_HEADS * 32) ** -0.5, MUL, after=[r])
                bank_free[STAT] = b2["wi"]
            later(turn_wi)
            return t

        def token_major(name, src, dst, width, after):
            def turn_values():
                for n in range(NB):
                    for c in range(width // P):
                        r = transpose(banks[STAT][:, (n * (width // P) + c) * P:(n * (width // P) + c + 1) * P],
                                      src[:, c, n * P:(n + 1) * P], ident, [after, bank_free[STAT]], signal=True)
                b2[name] = act(dst, banks[STAT][:, 0:NB * width], ACT.Copy, [r])
                bank_free[STAT] = b2[name]
            later(turn_values)

        def vm_reader(i):
            def read(bank, tok):
                t = scaled(vT[:, i, :], bank, tok, norm_m)
                if i == 1:
                    token_major("vmtok", vT, vmtok[:].rearrange("p n c -> p (n c)"), 2 * P, t)
                return t
            return read

        def v_reader(bank, tok):
            t = scaled(vT[:, 0, :], bank, tok, extra=[b2["vmtok"]])
            token_major("vtok", vT, vtok2[:].rearrange("p n c -> p (n c)"), P, t)
            return t

        def cg_reader(i):
            return plain(("cg", i), CG[:, i, :])

        def u_reader(i):
            def read(bank, tok):
                t = scaled(ctmp[:], bank, tok, extra=[b2.get("ctmp_free")])
                r = tt(cpad[:, 2:], ctmp[:], CG[:, i, :], MUL, [t, b2[("cg", i)], b2.get("cpad_free"), b2["cpad0"]])
                b2["ctmp_free"] = r
                r = conv_tile(i, T2, 3, cpad[:], ccv[:, i, :], lambda k: vcol("short", 3 * k + i), None, [r])
                b2["cpad_free"] = b2[("ccv", i)] = r
                return t
            return read

        def bg_reader(i):
            def read(bank, tok):
                t = scaled(ctmp[:], bank, tok, extra=[b2.get("ctmp_free")])
                r = tt(ccv[:, i, :], ccv[:, i, :], ctmp[:], MUL, [t, b2[("ccv", i)]])
                b2["ctmp_free"] = r
                b2[("yc", i)] = parts_of(i, ccv[:, i, :], YCH, YCL, r, T2)
                return t
            return read

        def gate_reader(m):
            def read(bank, tok):
                t = scaled(G2[:, m, :], bank, tok)
                b2[("gate", m)] = act(G2[:, m, :], G2[:, m, :], ACT.Tanh, [t, t_bgate], scale=0.5,
                                      bias=vcol("b_gate", m))
                return t
            return read

        def wcols(col, n):
            return columns(A["w_in_2"], col, n)

        def pairs(*tiles):
            c0, pieces, parts = 0, [], []
            for key, cols, M, reader in tiles:
                for off, w, col in cols:
                    pieces.append((c0 + off, w, wcols(col, w)))
                parts.append((key, c0, M, reader))
                c0 += M
            return Slab(KD, c0, pieces, xin2, T2, parts)

        def q_tile(r):
            return (("q", r), [(0, 64, C2_Q + 64 * r), (64, 64, C2_Q + 64 * (3 + r))], P,
                    roped(("q", r), qT[:, r, :], "rot_a", "cos_a", "sin_a"))

        def tile_(key, col, reader):
            return (key, [(0, P, col)], P, reader)

        xm = (MEMH, MEML, 0, 0, norm_m.tokens)
        mem_slabs = [slab2(A["w_mem_kv_2"], 0, [plain(("km", i), kmT[:, i, :], norm_m) for i in range(2)], "km", xm, T2),
                     slab2(A["w_mem_kv_2"], 256, [vm_reader(i) for i in range(2)], "vm", xm, T2)]
        in2 = [
            pairs(*[tile_(("qi", t), C2_QI + P * t, roped(("qi", t), qiT[:, t, :], "rot_i", "cos_i", "sin_i"))
                    for t in range(2)]),
            pairs(("ki", [(32 * i, 32, C2_KI) for i in range(4)], P, roped("ki", kiT[:], "rot_i", "cos_i", "sin_i")),
                  ("wi", [(0, IDX_HEADS, C2_WI)], IDX_HEADS, wi_reader)),
            pairs(q_tile(0), q_tile(1)),
            pairs(q_tile(2), tile_("k", C2_K, roped("k", kT[:], "rot_a", "cos_a", "sin_a"))),
            pairs(tile_("v", C2_V, v_reader), tile_("cg0", C2_CG, cg_reader(0))),
            pairs(*[tile_(("qc", t), C2_QC + P * t, plain(("qc", t), qcT[:, t, :])) for t in range(2)]),
            pairs(tile_("u0", C2_U, u_reader(0)), tile_("cg1", C2_CG + P, cg_reader(1))),
            pairs(tile_("u1", C2_U + P, u_reader(1)), tile_("cg2", C2_CG + 2 * P, cg_reader(2))),
            pairs(tile_("u2", C2_U + 2 * P, u_reader(2)), tile_("bg0", C2_BG, bg_reader(0))),
            pairs(tile_("bg1", C2_BG + P, bg_reader(1)), tile_("bg2", C2_BG + 2 * P, bg_reader(2))),
        ] + [pairs(*[tile_(("gate", m), C2_GATE + P * m, gate_reader(m)) for m in (2 * q, 2 * q + 1)]) for q in range(12)]

        def merge_reader(branch, m):
            def read(bank, tok):
                g = G2[:, branch * KD + m, :]
                if branch == 0:
                    t = stt(MG[:, m, :], g, 1.0, bank[:, 0:T2], ADD, MUL, [tok, b2[("gate", m)]])
                    b2[("mg", m)] = t
                    return t
                i = m % 2
                t = stt(mtmp[:, i, :], g, 1.0, bank[:, 0:T2], ADD, MUL, [tok, b2[("gate", branch * KD + m)], b2.get(("mtmp", i))])
                r = tt(MG[:, m, :], MG[:, m, :], mtmp[:, i, :], ADD, [t, b2[("mg", m)]])
                b2[("mtmp", i)] = b2[("mg", m)] = r
                if branch == 2:
                    merged[m] = parts_of(m, MG[:, m, :], MGH, MGL, r, T2, scale=0.5)
                return t
            return read

        merged, ya, yc, ym = [None] * KD, [None] * 3, [None] * 3, [None] * 2
        out2 = []
        for half in range(2):
            c, ms = 512 * half, range(4 * half, 4 * half + 4)
            att = A["w_att_out_2"].rearrange("(g r p) n -> g p r n", g=2, r=3)
            out2.append(Slab(3, 512, [(0, 512, att[g, :, :, c:c + 512], 64 * g, 64 * g + 64) for g in range(2)],
                             (YAH, YAL, 0, 0, ya), T2, [(("at", m), P * (m % 4), P, merge_reader(0, m)) for m in ms]))
            out2.append(Slab(3, 512, [(0, 512, columns(A["w_conv_out_2"], c, 512, 0, 3))],
                             (YCH, YCL, 0, 0, yc), T2, [(("co", m), P * (m % 4), P, merge_reader(1, m)) for m in ms]))
            out2.append(Slab(2, 512, [(0, 512, columns(A["w_mem_out_2"], c, 512, 0, 2))],
                             (YMH, YML, 0, 0, ym), T2, [(("me", m), P * (m % 4), P, merge_reader(2, m)) for m in ms]))

        def add2_reader(m, nxt):
            def read(bank, tok):
                t = tt(H2[m], bank[:, 0:T2], H2[m], ADD, [tok])
                nxt.tile(m, H2[m], t)
                return t
            return read
        wo2 = [slab2(A["w_o_2"], 256 * q, [add2_reader(2 * q + i, norm_h) for i in range(2)], ("wo2", q),
                     (MGH, MGL, 0, 0, merged), T2) for q in range(4)]
        norm_o = Sums(T2)
        norm_o.factor, norm_o.bank = rstd, STAT
        ffn_mem2 = dict(ffn_mem)
        up2, down2 = ffn("f2", T2, A["w_up_2"], A["w_down_2"], "f2_conv", None, norm_h,
                         (XH, XL, 0, 0, norm_h.tokens), lambda m: add2_reader(m, norm_o), ffn_mem2)

        def attend_unit(qs, ks, vals, r, e, n, penalty, hi, lo, key, results):
            half = slice(64 * e, 64 * e + 64)
            pt = PT[:, e, :]
            S = (n + 1) * P if penalty else T2
            i, b = 2 * e + n, 3 + n
            pr = prob[:, i, 0:S]
            mx, nm, sm, rc = (soft[:, i, c:c + 1] for c in range(4))
            lg = banks[b][:, 0:S]
            t = mm(lg, qs[half, n * P:(n + 1) * P], ks[half, 0:S], True, True, [bank_free[b], *key], signal=True)
            yield
            if penalty:
                a = put("dve", lambda e_: e_.tensor_tensor_reduce(pr, lg, pen[:, n, 0:S], 1.0, -3.0e38, ADD, MAX, mx),
                        [t, b2[("pen", n)], b2.get(("prob", i))])
                bank_free[b] = a
                src = pr
            else:
                a = put("dve", lambda e_: e_.reduce_max(mx, lg, AX.X), [t, b2.get(("prob", i))])
                src = lg
            a = ts(nm, mx, -(64 ** -0.5), MUL, after=[a])
            yield
            a = act(pr, src, ACT.Exp, [a, b2.get(("prob", i))], scale=64 ** -0.5, bias=nm, accum=sm)
            if not penalty:
                bank_free[b] = a
            yield
            yield
            a = put("dve", lambda e_: e_.reciprocal(rc, sm), [a])
            a = ts(pr, pr, rc, MUL, after=[a])
            yield
            yield
            for kb in range(S // P):
                col = kb * T2 + n * P if not (penalty and kb) else T2
                t = transpose(banks[5][:, col:col + P], prob[:, i, kb * P:(kb + 1) * P], ident,
                              [a, bank_free[5] if n == 0 else None], signal=True)
            b2[("prob", i)] = t
            if n == 0:
                return
            w = 3 * P if penalty else 4 * P
            c = act(pt[:, 0:w], banks[5][:, 0:w], ACT.Copy, [t, b2.get(("pt", e))])
            bank_free[5] = c
            yield
            yield
            vcols = slice(64 * e, 64 * e + 64)
            mm(banks[6][half, 0:T2], vals[:, 0, vcols], pt[:, 0:T2], True, False, [c, bank_free[6], b2["vtok"]])
            if penalty:
                t = mm(banks[6][half, P:T2], vals[:, 1, vcols], pt[:, T2:T2 + P], False, True, signal=True)
            else:
                t = mm(banks[6][half, 0:T2], vals[:, 1, vcols], pt[:, T2:2 * T2], False, True, signal=True)
            b2[("pt", e)] = t
            if e == 1:
                results[r] = parts_of(r, banks[6][:, 0:T2], hi, lo, t, T2)
                bank_free[6] = results[r][1]

        def attend(*units):
            active, waiting, since = [], list(units), 4
            while active or waiting:
                if waiting and since >= 4:
                    active.append(waiting.pop(0))
                    since = 0
                for u in list(active):
                    if next(u, "end") == "end":
                        active.remove(u)
                since += 1
                yield

        def attention():
            while "wi" not in b2 or "ki" not in b2 or ("qi", 1) not in b2:
                yield
            for n in range(NB):
                S = (n + 1) * P
                acc = None
                for t_ in range(2):
                    for h in range(4):
                        rows = slice(32 * h, 32 * h + 32)
                        t = mm(banks[3 + h][:, 0:S], qiT[rows, t_, n * P:(n + 1) * P], kiT[rows, 0:S], True, True,
                               [b2[("qi", t_)], b2["ki"], bank_free[3 + h]], signal=True)
                        a = act(relu[:, h, 0:S], banks[3 + h][:, 0:S], ACT.Relu, [t, b2.get(("relu", h))])
                        bank_free[3 + h] = a
                        w = wiT[:, n * IDX_HEADS + 4 * t_ + h:n * IDX_HEADS + 4 * t_ + h + 1]
                        if acc is None:
                            acc = ts(sco[:, n, 0:S], relu[:, h, 0:S], w, MUL, after=[a, b2["wi"]])
                        else:
                            acc = stt(sco[:, n, 0:S], relu[:, h, 0:S], w, sco[:, n, 0:S], MUL, ADD, [a, acc])
                        b2[("relu", h)] = acc
                        if h % 2:
                            yield
                dg = sco[:, n, n * P:S]
                acc = put("pool", lambda e, dg=dg: e.affine_select(out=dg, in_=dg, compare_op=ALU.is_ge, fill=FILL, base=0,
                                                                   pattern=[[-1, P]], channel_multiplier=1), [acc])
                b2[("sco", n)] = acc
            for n in range(NB):
                S = (n + 1) * P
                a = b2[("sco", n)]
                s_ = sco[:, n, 0:S]
                for r in range(TOPK // 8):
                    a = put("dve", lambda e, s_=s_: e.max(max8[:], s_), [a])
                    a = put("dve", lambda e, s_=s_: e.match_replace(s_, max8[:], s_, TAKEN), [a])
                    yield
                    yield
                a = ts(pen[:, n, 0:S], s_, TAKEN, ALU.not_equal, PENALTY, MUL, after=[a])
                dg = pen[:, n, n * P:S]
                b2[("pen", n)] = put("pool", lambda e, dg=dg: e.affine_select(
                    out=dg, in_=dg, compare_op=ALU.is_ge, fill=PENALTY, base=0, pattern=[[-1, P]],
                    channel_multiplier=1), [a])
            while "k" not in b2 or "vtok" not in b2:
                yield
            yield from attend(*(attend_unit(qT[:, r, :], kT[:], vtok2, r, e, n, True, YAH, YAL, [b2["k"], b2[("q", r)]], ya)
                                for r in range(3) for e in range(2) for n in range(NB)))
            while ("qc", 1) not in b2:
                yield
            yield from attend(*(attend_unit(qcT[:, r, :], kmT[:, r, :], vmtok[:, :, r * P:(r + 1) * P], r, e, n, False,
                                            YMH, YML, [b2[("km", r)], b2[("qc", r)], b2["vmtok"]], ym)
                                for r in range(2) for e in range(2) for n in range(NB)))

        def start2():
            norm_f.finish()
            t = None
            for k in range(KD):
                t = stt(H2[k], H2[k], vcol("final1", k), rstd[:, 0:T2], MUL, MUL, [norm_f.rstd, t_vec])
                last_rstd_use[0] = t
                norm_g.tile(k, H2[k], t, adder="pool", ticks=50)
                yield
        gens = {}
        run(dt_slab)
        dt_gen = m2_dt()
        background.append(dt_gen)
        for p in range(4):
            sf, sq_, si, sg_ = hg_slabs[p]
            run(sf)
            gates = hg_gates(p)
            background.append(gates)
            run(sq_)
            def q_silu(p=p):
                yield
                a = act(qth[:], q_[:], ACT.Tanh, [hg[("q", p, 0)], hg[("q", p, 1)], hg.get("qth_free")])
                yield
                b = stt(q_[:], qth[:], 1.0, q_[:], ADD, MUL, [a])
                hg["qth_free"] = b
                hg[("qa", p)] = (a, b)
            background.append(q_silu())
            run(si)
            finish(gates, dt_gen)
            if p:
                finish(*gens[p - 1])
            def pair_of(p):
                for j in range(2):
                    yield from hg_head(p, j)
            gens[p] = [pair_of(p)]
            background.extend(gens[p])
            run(sg_)
            for j in range(2):
                h = 2 * p + j
                a = act(qth[:, 0:T1], G_all[:, h, :], ACT.Tanh, [hg[("g", p, j)], hg.get("qth_free")])
                hg[("ga", h)] = stt(G_all[:, h, :], qth[:, 0:T1], 1.0, G_all[:, h, :], ADD, MUL, [a])
                hg["qth_free"] = hg[("ga", h)]
        m2_gen = m2_scores()
        run(b_slab)
        run(c_slab)
        background.append(m2_gen)
        parts_a = hg_parts()
        background.append(parts_a)
        for s in z_slabs:
            run(s)
        finish(*gens[3], parts_a)
        for k in range(8):
            mixA[k] = hg[("mix", k)]
        tiles = m2_heads()
        background.append(tiles)
        for kind, q, s in m2_order:
            while kind in "zx" and q >= 2 and ("tile_done", 2 * q - 3) not in m2:
                tick(1)
            run(s)
        finish(m2_gen, tiles)
        while ("group_done", 1) not in m2:
            tick(1)
        for k in range(8):
            mixB[k] = m2[("mix", k)]
        main_banks[:] = [0, 1, 2, 3]
        for s in outB:
            run(s)
        ffn_mem["start"] = (done["dve"], count["dve"])
        ffn_mem["start2"] = (done["pe"], count["pe"])
        ffn_mem["t_pad"] = [memset(ffn_mem["pad"][:, i, 0:2], 0.0, [ffn_mem["start"], ffn_mem["start2"], (done["act"], count["act"])])
                            for i in range(4)]
        up1[0].hook = norm2.finish
        s_mem = semaphore("s_mem")
        t_mem = dma(MEMR[:], A["memT"].rearrange("(k p) t -> p k t", p=P), s_mem, ffn_mem["t_pad"], engine="act")

        def mem_norm():
            for k in range(KD):
                norm_m.tile(k, MEMR[:, k, :], t_mem, ticks=12)
                for _ in range(5):
                    yield
            while norm_m.sum[0] is None:
                yield
            norm_m.finish()
        for s in up1:
            run(s)
        mem_gen = mem_norm()
        background.append(mem_gen)
        for s in down1:
            run(s)
        finish(mem_gen)
        main_banks[:] = [0, 1, 2]
        over_ = [(done["pe"], count["pe"]), (done["act"], count["act"]), (done["dve"], count["dve"])]
        t_con2[0] = dma(con2[:], A["con"][:, NCON1:NCON], semaphore("s_con2"), over_, engine="act")
        b2["cpad0"] = memset(cpad[:, 0:2], 0.0, over_)
        start2_gen = start2()
        mem_slabs[0].early = lambda: background.append(start2_gen)
        for s in mem_slabs:
            run(s)
        finish(start2_gen)
        in2[0].hook = norm_g.finish
        att_gen = attention()
        background.append(att_gen)
        for s in in2:
            run(s)
        finish(att_gen)
        for i in range(3):
            yc[i] = b2[("yc", i)]
        main_banks[:] = [0, 1, 2, 3, 4, 5]
        for s in out2:
            run(s)
        main_banks[:] = [0, 1, 2, 3]
        for s in wo2:
            run(s)
        over_ = [(done["pe"], count["pe"]), (done["act"], count["act"]), (done["dve"], count["dve"])]
        ffn_mem2["start"] = over_[2]
        ffn_mem2["t_pad"] = [memset(ffn_mem["pad"][:, i, 0:2], 0.0, over_) for i in range(4)]
        up2[0].hook = norm_h.finish
        for s in up2:
            run(s)
        for s in down2:
            run(s)
        flush()
        norm_o.finish()
        s_out = semaphore("s_out")
        out_k = out.rearrange("(k p) t -> k p t", p=P)
        for k in range(KD):
            t = stt(H2[k], H2[k], vcol("g_final", k), rstd[:, 0:T2], MUL, MUL, [norm_o.rstd, t_vec])
            t = dma(out_k[k], H2[k], s_out, [t])
        queues["sp"].append((None, [t], None, 0))
        block = ctx.enter_context(nc.Block())

        def emit(engine, name):
            seen = {}
            for issue, waits, sem, inc in queues[name]:
                need = {}
                for s, v in waits:
                    if seen.get(id(s), 0) < v:
                        need[id(s)] = (s, max(v, need.get(id(s), (s, 0))[1]))
                for i, (s, v) in need.items():
                    engine.wait_ge(s, v)
                    seen[i] = v
                if issue is None:
                    continue
                ins = issue(engine)
                if sem is not None:
                    ins.then_inc(sem, inc)

        @block.sync
        def _(e):
            emit(e, "sp")

        @block.tensor
        def _(e):
            emit(e, "pe")

        @block.scalar
        def _(e):
            emit(e, "act")

        @block.vector
        def _(e):
            emit(e, "dve")

        @block.gpsimd
        def _(e):
            emit(e, "pool")


def kernel(**inputs):
    import concourse.bacc as bacc
    from concourse import mybir
    from concourse.bass_utils import run_bass_kernel_spmd

    a = {n: np.asarray(v) for n, v in inputs.items()}

    def rows(x):
        return np.reshape(x, (-1, P)).T

    laid = {
        "hT": np.concatenate([a["meta_tokens"], a["x"][0]], axis=0).T,
        "memT": a["mem_2"][0].T,
        "vec": np.concatenate([
            rows(a["norm1_w"]), rows(a["hg_norm_w"]), rows(a["m2_conv_w"]), rows(a["m2_conv_b"]), rows(a["m2_norm_w"]),
            rows(np.repeat(a["m2_d"][0], 64)), rows(a["norm2_w"]), rows(a["final_norm_w"]), rows(a["ffn_conv_w"]),
            rows(a["ffn_conv_b"]), rows(a["hg_lb_logits"]), rows(a["b_gate_2"]), rows(a["conv_w_short_2"]),
            rows(a["g_mix_2"]), rows(a["g_mem_2"]), rows(a["g_ffn_2"]), rows(a["conv_w_ffn_2"]), rows(a["g_final_2"]),
        ], axis=1),
        "heads": np.stack([a["m2_dt_bias"][0], a["m2_a_log"][0]], axis=1),
    }
    laid["con"], laid["chunk_mask"] = constants()
    for n in ("w_in", "w_out", "ffn_w_up", "ffn_w_down", "w_in_2", "w_att_out_2", "w_conv_out_2", "w_mem_out_2",
              "w_o_2", "w_mem_kv_2", "w_up_2", "w_down_2"):
        laid[n] = a[n][0]
    nc = bacc.Bacc("TRN2", target_bir_lowering=False, num_devices=1)
    arrays, aps = {}, {}
    for n, v in laid.items():
        v = np.ascontiguousarray(v)
        arrays[f"in_{n}"] = v
        aps[n] = nc.dram_tensor(f"in_{n}", v.shape, mybir.dt.from_np(v.dtype), kind="ExternalInput").ap()
    out = nc.dram_tensor("out_T", (D, T2), mybir.dt.float32, kind="ExternalOutput").ap()
    build_program(nc, aps, out)
    r = run_bass_kernel_spmd(nc, [arrays], core_ids=[0])
    return np.ascontiguousarray(r.results[0]["out_T"].T)[None]
```
